# Optimizing a Trainium2 kernel written in Bass

```python
import jax, jax.numpy as jnp
from jax import lax
import numpy as np

D_MODEL = 2048
BATCH = 1
SEQ = 512
DEPTH = 1
DEC_BATCH = 8
DEC_SEQ = 8
PAST_LEN = 2048
PAGE_SIZE = 128

A_WINDOWS = (128, 512, 2048)
A_DILATIONS = (1, 4, 16)
A_GROUPS = 3
A_HEADS = 8
A_HEAD_DIM = 128
A_WIDTH = A_HEADS * A_HEAD_DIM
A_QBLOCK = 128
ATT_SCALE = A_HEAD_DIM ** -0.5
SSM_D_INNER = D_MODEL
SSM_HEAD_DIM = 64
SSM_HEADS = SSM_D_INNER // SSM_HEAD_DIM
SSM_GROUPS = 8
SSM_D_STATE = 128
SSM_CONV_W = 4
SSM_CHUNK = 128
SSM_CONV_DIM = SSM_D_INNER + 2 * SSM_GROUPS * SSM_D_STATE
QKV_WIDTH = A_GROUPS * A_WIDTH
IN_SPLITS = (QKV_WIDTH, QKV_WIDTH, QKV_WIDTH, A_WIDTH, SSM_D_INNER, SSM_CONV_DIM, SSM_HEADS, D_MODEL, D_MODEL)
IN_WIDTH = sum(IN_SPLITS)
NORM_EPS = 1e-6

kernel_name = "hybrid_dilated_attn_ssd_step"

def _rmsnorm(x, g):
    xf = x.astype(jnp.float32)
    y = xf * lax.rsqrt(jnp.mean(xf * xf, axis=-1, keepdims=True) + NORM_EPS)
    return (y * g.astype(jnp.float32)).astype(x.dtype)

def _masked_softmax_lse(scores, mask):
    s = jnp.where(mask, scores, -jnp.inf)
    m = jnp.max(s, axis=-1, keepdims=True)
    e = jnp.exp(s - m)
    z = jnp.sum(e, axis=-1, keepdims=True)
    return e / z, (m + jnp.log(z))[..., 0]

def _dilated_attn_prompt(q, k, v, window, dilation):
    bsz, s, h, e = q.shape
    nk = window // dilation
    L = s // dilation
    qb = A_QBLOCK
    nb = -(-L // qb)
    lp = nb * qb

    def to_sub(t):
        return t.reshape(bsz, L, dilation, h, e).transpose(0, 2, 1, 3, 4)

    qs = jnp.pad(to_sub(q), ((0, 0), (0, 0), (0, lp - L), (0, 0), (0, 0))).reshape(bsz, dilation, nb, qb, h, e)
    kpad = ((0, 0), (0, 0), (nk, lp - L), (0, 0), (0, 0))
    ks = jnp.pad(to_sub(k), kpad)
    vs = jnp.pad(to_sub(v), kpad)
    kj = jnp.arange(qb + nk)
    idx = jnp.arange(nb)[:, None] * qb + kj[None, :]
    kb = ks[:, :, idx]
    vb = vs[:, :, idx]
    scores = jnp.einsum('bdnqhe,bdnkhe->bdnhqk', qs, kb, preferred_element_type=jnp.float32) * ATT_SCALE
    dist = jnp.arange(qb)[:, None] + nk - kj[None, :]
    key_sub = idx[:, None, :] - nk
    mask = (dist >= 0) & (dist <= nk) & (key_sub >= 0)
    p, lse = _masked_softmax_lse(scores, mask[None, None, :, None])
    o = jnp.einsum('bdnhqk,bdnkhe->bdnqhe', p.astype(vb.dtype), vb, preferred_element_type=jnp.float32)
    o = o.reshape(bsz, dilation, lp, h, e)[:, :, :L].transpose(0, 2, 1, 3, 4).reshape(bsz, s, h, e)
    lse = lse.transpose(0, 1, 2, 4, 3).reshape(bsz, dilation, lp, h)[:, :, :L]
    lse = lse.transpose(0, 2, 1, 3).reshape(bsz, s, h)
    return o, lse

def _dilated_attn_decode(q, k_new, v_new, kv_buf, window, dilation):
    wb = kv_buf.shape[1]
    t = q.shape[1]
    nk = window // dilation
    k_ctx = jnp.concatenate([kv_buf[:, :, 0], k_new], axis=1)
    v_ctx = jnp.concatenate([kv_buf[:, :, 1], v_new], axis=1)
    idx = wb + jnp.arange(t)[:, None] - jnp.arange(nk + 1)[None, :] * dilation
    valid = idx >= 0
    idxc = jnp.maximum(idx, 0)
    kg = k_ctx[:, idxc]
    vg = v_ctx[:, idxc]
    scores = jnp.einsum('bthe,btkhe->bthk', q, kg, preferred_element_type=jnp.float32) * ATT_SCALE
    p, lse = _masked_softmax_lse(scores, valid[None, :, None, :])
    o = jnp.einsum('bthk,btkhe->bthe', p.astype(vg.dtype), vg, preferred_element_type=jnp.float32)
    new_buf = jnp.concatenate([kv_buf, jnp.stack([k_new, v_new], axis=2)], axis=1)[:, t:]
    return o, lse, new_buf

def _ssd(xs, dt, a, bm, cm, h0):
    f32 = jnp.float32
    bsz, l, nh, p = xs.shape
    g, n = bm.shape[2], bm.shape[3]
    r = nh // g
    chunk = SSM_CHUNK if l % SSM_CHUNK == 0 else l
    nc = l // chunk
    xdt = (xs.astype(f32) * dt[..., None]).reshape(bsz, nc, chunk, g, r, p)
    bc = bm.astype(f32).reshape(bsz, nc, chunk, g, n)
    cc = cm.astype(f32).reshape(bsz, nc, chunk, g, n)
    da = (dt * a).reshape(bsz, nc, chunk, g, r).transpose(0, 3, 4, 1, 2)
    cs = jnp.cumsum(da, axis=-1)
    tri = jnp.tril(jnp.ones((chunk, chunk), dtype=bool))
    decay = jnp.exp(jnp.where(tri, cs[..., :, None] - cs[..., None, :], -jnp.inf))
    cb = jnp.einsum('bclgn,bcsgn->bgcls', cc, bc)
    y_diag = jnp.einsum('bgcls,bgrcls,bcsgrp->bclgrp', cb, decay, xdt)
    decay_states = jnp.exp(cs[..., -1:] - cs)
    states = jnp.einsum('bcsgn,bgrcs,bcsgrp->bcgrpn', bc, decay_states, xdt)
    states = jnp.concatenate([h0.astype(f32).reshape(bsz, 1, g, r, p, n), states], axis=1)
    cz = jnp.cumsum(jnp.pad(cs[..., -1], ((0, 0), (0, 0), (0, 0), (1, 0))), axis=-1)
    tri_c = jnp.tril(jnp.ones((nc + 1, nc + 1), dtype=bool))
    decay_chunk = jnp.exp(jnp.where(tri_c, cz[..., :, None] - cz[..., None, :], -jnp.inf))
    new_states = jnp.einsum('bgrzc,bcgrpn->bzgrpn', decay_chunk, states)
    y_off = jnp.einsum('bclgn,bcgrpn,bgrcl->bclgrp', cc, new_states[:, :-1], jnp.exp(cs))
    y = (y_diag + y_off).reshape(bsz, l, nh, p)
    final = new_states[:, -1].reshape(bsz, nh, p, n).astype(h0.dtype)
    return y, final

def _layer(x, c, kv_bufs, conv_state, ssm_state, decode,
           w_ada, b_ada, g_pre, g_post, w_in, conv_w, conv_b, dt_bias, a_log, d_skip, g_ssm, w_o_a, w_o_b, w_o):
    bsz, l, _ = x.shape
    mod = jax.nn.silu(c) @ w_ada + b_ada
    shift, scale, gate = jnp.split(mod, 3, axis=-1)
    h = _rmsnorm(x, g_pre) * (1 + scale[:, None]) + shift[:, None]
    proj = h @ w_in
    cuts = [int(i) for i in np.cumsum(IN_SPLITS)[:-1]]
    q, k, v, z_a, z_b, xbc, dt_raw, r_a, r_b = jnp.split(proj, cuts, axis=-1)

    q = q.reshape(bsz, l, A_GROUPS, A_HEADS, A_HEAD_DIM)
    k = k.reshape(bsz, l, A_GROUPS, A_HEADS, A_HEAD_DIM)
    v = v.reshape(bsz, l, A_GROUPS, A_HEADS, A_HEAD_DIM)
    outs, lses, new_bufs = [], [], []
    for gi in range(A_GROUPS):
        w, d = A_WINDOWS[gi], A_DILATIONS[gi]
        qg, kg, vg = q[:, :, gi], k[:, :, gi], v[:, :, gi]
        if decode:
            o, lse, nbuf = _dilated_attn_decode(qg, kg, vg, kv_bufs[gi], w, d)
        else:
            o, lse = _dilated_attn_prompt(qg, kg, vg, w, d)
            nbuf = jnp.stack([kg, vg], axis=2)[:, -min(w, l):]
        outs.append(o)
        lses.append(lse)
        new_bufs.append(nbuf)
    wts = jax.nn.softmax(jnp.stack(lses, axis=0), axis=0)
    o_a = jnp.sum(wts[..., None] * jnp.stack(outs, axis=0), axis=0)
    o_a = o_a.reshape(bsz, l, A_WIDTH).astype(x.dtype) * jax.nn.silu(z_a)
    p_a = o_a @ w_o_a

    ext = jnp.concatenate([conv_state, xbc], axis=1)
    conv = conv_b
    for kk in range(SSM_CONV_W):
        conv = conv + conv_w[kk] * ext[:, kk:kk + l]
    new_conv = ext[:, l:]
    xbc_act = jax.nn.silu(conv)
    xs, bm, cm = jnp.split(xbc_act, [SSM_D_INNER, SSM_D_INNER + SSM_GROUPS * SSM_D_STATE], axis=-1)
    xs = xs.reshape(bsz, l, SSM_HEADS, SSM_HEAD_DIM)
    bm = bm.reshape(bsz, l, SSM_GROUPS, SSM_D_STATE)
    cm = cm.reshape(bsz, l, SSM_GROUPS, SSM_D_STATE)
    dt = jax.nn.softplus(dt_raw.astype(jnp.float32) + dt_bias.astype(jnp.float32))
    a = -jnp.exp(a_log.astype(jnp.float32))
    y, new_ssm = _ssd(xs, dt, a, bm, cm, ssm_state)
    y = y + xs.astype(jnp.float32) * d_skip.astype(jnp.float32)[:, None]
    yg = y.reshape(bsz, l, SSM_D_INNER) * jax.nn.silu(z_b.astype(jnp.float32))
    yg = yg.reshape(bsz, l, SSM_GROUPS, SSM_D_INNER // SSM_GROUPS)
    yg = yg * lax.rsqrt(jnp.mean(yg * yg, axis=-1, keepdims=True) + NORM_EPS)
    yn = (yg.reshape(bsz, l, SSM_D_INNER) * g_ssm.astype(jnp.float32)).astype(x.dtype)
    p_b = yn @ w_o_b

    merged = jax.nn.sigmoid(r_a) * p_a + jax.nn.sigmoid(r_b) * p_b
    out = merged @ w_o
    y_out = x + gate[:, None] * _rmsnorm(out, g_post)
    return y_out, new_bufs, new_conv, new_ssm

def setup_inputs(seed: int = 0) -> dict:
    key = jax.random.key(seed)
    ks = jax.random.split(key, 24)
    f32 = jnp.float32

    def nrm(k, shape, s):
        return jax.random.normal(k, shape, f32) * s

    wb = [min(w, PAST_LEN) for w in A_WINDOWS]
    kv_shape = lambda n: (DEPTH, DEC_BATCH, n, 2, A_HEADS, A_HEAD_DIM)
    dt0 = jnp.exp(jax.random.uniform(ks[15], (DEPTH, SSM_HEADS), f32, np.log(1e-3), np.log(1e-1)))
    return {
        "x_prompt": nrm(ks[0], (BATCH, SEQ, D_MODEL), 1.0),
        "x_sample": nrm(ks[1], (DEC_BATCH, DEC_SEQ, D_MODEL), 1.0),
        "cache_a_w128": nrm(ks[2], kv_shape(wb[0]), 1.0),
        "cache_a_w512": nrm(ks[3], kv_shape(wb[1]), 1.0),
        "cache_a_w2048": nrm(ks[4], kv_shape(wb[2]), 1.0),
        "state_conv": nrm(ks[5], (DEPTH, DEC_BATCH, SSM_CONV_W - 1, SSM_CONV_DIM), 1.0),
        "state_ssm": nrm(ks[6], (DEPTH, DEC_BATCH, SSM_HEADS, SSM_HEAD_DIM, SSM_D_STATE), 0.1),
        "c_prompt": nrm(ks[7], (BATCH, D_MODEL), 1.0),
        "c_sample": nrm(ks[8], (DEC_BATCH, D_MODEL), 1.0),
        "w_ada": nrm(ks[9], (DEPTH, D_MODEL, 3 * D_MODEL), 0.2 * D_MODEL ** -0.5),
        "b_ada": nrm(ks[10], (DEPTH, 3 * D_MODEL), 0.01),
        "g_pre": 1.0 + nrm(ks[11], (DEPTH, D_MODEL), 0.05),
        "g_post": 1.0 + nrm(ks[12], (DEPTH, D_MODEL), 0.05),
        "w_in": nrm(ks[13], (DEPTH, D_MODEL, IN_WIDTH), D_MODEL ** -0.5),
        "conv_w": nrm(ks[14], (DEPTH, SSM_CONV_W, SSM_CONV_DIM), SSM_CONV_W ** -0.5),
        "conv_b": nrm(ks[16], (DEPTH, SSM_CONV_DIM), 0.01),
        "dt_bias": dt0 + jnp.log(-jnp.expm1(-dt0)),
        "a_log": jnp.log(jax.random.uniform(ks[17], (DEPTH, SSM_HEADS), f32, 1.0, 16.0)),
        "d_skip": 1.0 + nrm(ks[18], (DEPTH, SSM_HEADS), 0.05),
        "g_ssm": 1.0 + nrm(ks[19], (DEPTH, SSM_D_INNER), 0.05),
        "w_o_a": nrm(ks[20], (DEPTH, A_WIDTH, D_MODEL), A_WIDTH ** -0.5),
        "w_o_b": nrm(ks[21], (DEPTH, SSM_D_INNER, D_MODEL), SSM_D_INNER ** -0.5),
        "w_o": nrm(ks[22], (DEPTH, D_MODEL, D_MODEL), D_MODEL ** -0.5),
    }

def reference(x_prompt, x_sample, cache_a_w128, cache_a_w512, cache_a_w2048, state_conv, state_ssm,
              c_prompt, c_sample, w_ada, b_ada, g_pre, g_post, w_in, conv_w, conv_b, dt_bias, a_log,
              d_skip, g_ssm, w_o_a, w_o_b, w_o):
    y_prompt, y_sample = x_prompt, x_sample
    pk128, pk512, pk2048, pconv, pssm = [], [], [], [], []
    sk128, sk512, sk2048, sconv, sssm = [], [], [], [], []
    for i in range(DEPTH):
        lw = (w_ada[i], b_ada[i], g_pre[i], g_post[i], w_in[i], conv_w[i], conv_b[i], dt_bias[i], a_log[i],
              d_skip[i], g_ssm[i], w_o_a[i], w_o_b[i], w_o[i])
        b_p = x_prompt.shape[0]
        conv0 = jnp.zeros((b_p, SSM_CONV_W - 1, SSM_CONV_DIM), x_prompt.dtype)
        ssm0 = jnp.zeros((b_p, SSM_HEADS, SSM_HEAD_DIM, SSM_D_STATE), x_prompt.dtype)
        y_prompt, bufs_p, conv_p, ssm_p = _layer(y_prompt, c_prompt, None, conv0, ssm0, False, *lw)
        y_sample, bufs_s, conv_s, ssm_s = _layer(
            y_sample, c_sample, (cache_a_w128[i], cache_a_w512[i], cache_a_w2048[i]),
            state_conv[i], state_ssm[i], True, *lw)
        pk128.append(bufs_p[0]); pk512.append(bufs_p[1]); pk2048.append(bufs_p[2])
        pconv.append(conv_p); pssm.append(ssm_p)
        sk128.append(bufs_s[0]); sk512.append(bufs_s[1]); sk2048.append(bufs_s[2])
        sconv.append(conv_s); sssm.append(ssm_s)
    p_kv128, p_kv512, p_kv2048 = jnp.stack(pk128), jnp.stack(pk512), jnp.stack(pk2048)
    p_conv, p_ssm = jnp.stack(pconv), jnp.stack(pssm)
    s_kv128, s_kv512, s_kv2048 = jnp.stack(sk128), jnp.stack(sk512), jnp.stack(sk2048)
    s_conv, s_ssm = jnp.stack(sconv), jnp.stack(sssm)
    return (y_prompt, y_sample, p_kv128, p_kv512, p_kv2048, p_conv, p_ssm, s_kv128, s_kv512, s_kv2048, s_conv, s_ssm)


_drawn_inputs = setup_inputs


def setup_inputs(seed=0):
    import zlib

    import numpy as np

    out = dict(_drawn_inputs(seed))
    spreads = {}
    factors = {'g_post': 8.0, 'conv_b': 3.402, 'd_skip': 8.0, 'g_ssm': 8.0, 'w_o_a': 4.46}
    for name, (base, spread) in spreads.items():
        noise = np.random.default_rng([zlib.crc32(name.encode()), seed]).standard_normal(out[name].shape)
        drawn = base * np.exp(spread * noise) if base else spread * noise
        out[name] = __import__('jax').numpy.asarray(drawn.astype(out[name].dtype))
    for name, factor in factors.items():
        out[name] = (out[name] * factor).astype(out[name].dtype)
    return out
```

```python
from contextlib import ExitStack

import concourse.bass as bass
from concourse import mybir

F32 = mybir.dt.float32
F32R = mybir.dt.float32r
ACT = mybir.ActivationFunctionType
ALU = mybir.AluOpType
AX = mybir.AxisListType.X
ds = bass.ds

P = 128
D = 2048
KT = D // P
SEQ = 512
NB = 8
NT = 8
SAMP = NB * NT
TOK = SEQ + SAMP
NSEQ = 1 + NB
GROUPS = ((128, 1), (512, 4), (2048, 16))
H = 8
E = 128
AW = H * E
QKV = 3 * AW
COL_K, COL_V, COL_ZA = QKV, 2 * QKV, 3 * QKV
COL_ZB = COL_ZA + AW
COL_XBC = COL_ZB + D
CONV = D + 2 * 8 * 128
COL_DT = COL_XBC + CONV
SH = 32
COL_R = COL_DT + SH
INW = COL_R + 2 * D
CW = 4
SG = 8
HALF = TOK // 2
BC = 256
EPS = 1e-6
SCALE = float(E) ** -0.5
MASK0 = SEQ + 3

SETS = [(2, c, (c,)) for c in range(8)] + [(1, c, (c, c + 4)) for c in range(4)] + [(0, 0, tuple(range(8)))]
NSETS = len(SETS)
NQ = sum(len(q) for _, _, q in SETS)


def shape_constants():
    import numpy as np
    neg = np.float32(-1e30)
    i = np.arange(P)
    prompt = np.zeros((P, MASK0 + 2 * P), np.float32)
    lag = 4 * i[:, None] + 3 - np.arange(MASK0)[None, :]
    prompt[:, :MASK0] = np.where((lag >= 0) & (lag <= 128), 0, neg)
    dist = i[:, None] - i[None, :]
    prompt[:, MASK0:MASK0 + P] = np.where(dist >= 0, 0, neg)
    prompt[:, MASK0 + P:] = np.where((dist >= 0) & (dist % 4 == 0), 0, neg)
    b, t = np.arange(SAMP) // NT, np.arange(SAMP) % NT
    samp = np.zeros((SAMP, 3 * P + 3 * SAMP), np.float32)
    for g, (_, d) in enumerate(GROUPS):
        first = (t - t % d) // d
        samp[:, g * P:(g + 1) * P] = np.where(i[None, :] >= first[:, None], 0, neg)
        lag = t[:, None] - t[None, :]
        ok = (b[:, None] == b[None, :]) & (lag >= 0) & (lag % d == 0)
        samp[:, 3 * P + g * SAMP:3 * P + (g + 1) * SAMP] = np.where(ok, 0, neg)
    causal = (i[:, None] <= i[None, :]).astype(np.float32)
    block = ((b[:, None] == b[None, :]) & (t[:, None] <= t[None, :])).astype(np.float32)
    owner = (b[:, None] == np.arange(NB)[None, :]).astype(np.float32)
    seg = np.ones((SH, TOK), np.float32)
    seg[:, 0:SEQ:P] = 0
    seg[:, SEQ:TOK:NT] = 0
    return {"seg": seg, "ident": np.eye(P, dtype=np.float32), "mask_prompt": prompt, "mask_samp": samp,
            "causal": causal, "block": block, "owner": owner}


class Mem:

    def __init__(self, nc, ctx):
        self.nc, self.ctx = nc, ctx
        self.sems = []

    def sb(self, name, shape, dt=F32):
        return self.ctx.enter_context(self.nc.sbuf_tensor(name, shape, dt))

    def ps(self, name, shape=(P, 512)):
        return self.ctx.enter_context(self.nc.psum_tensor(name, list(shape), F32))

    def sem(self, name):
        if not self.sems:
            self.ctx.callback(self.nc.all_engine_barrier)
            self.ctx.callback(lambda: self.nc.clear_and_free_semaphores(self.sems))
        self.sems.append(self.nc.alloc_semaphore(name=name))
        return self.sems[-1]



def phase_norm(nc, A, S, per):
    with ExitStack() as ctx:
        m = Mem(nc, ctx)
        crow = m.sb("crow", [NSEQ, D])
        sq = m.sb("sq", [P, D])
        cact = sq[0:NSEQ, :]
        cT = m.sb("cT", [P, KT, NSEQ])
        vrows = m.sb("vrows", [112, P])
        cwrows = m.sb("cwrows", [P, P])
        raw = m.sb("ada_raw", [P, 3, KT, BC])
        x = m.sb("x", [P, 5, D])
        ssq = m.sb("ssq", [P, 5])
        root = m.sb("root", [P, 5])
        rstd = m.sb("rstd", [P, 5])
        mod = m.sb("mod", [P, 2 * KT, NSEQ])
        amp = m.sb("amp", [P, KT, NSEQ])
        hF = m.sb("hF", [P, 2, TOK])
        eps = m.sb("eps_n", [P, 1])
        grow = m.sb("grow", [NSEQ, D])
        ps_c = m.ps("ps_c")
        ps_v = m.ps("ps_v")
        ps_m = [m.ps(f"ps_m{i}") for i in range(2)]
        mrow = m.sb("mrow", [NSEQ, 2, BC])
        bgate = m.sb("bgate", [NSEQ, D])
        ps_h = [m.ps(f"ps_h{i}", (P, 1024)) for i in range(2)]

        c_in, v_in, x_in = m.sem("c_in"), m.sem("v_in"), m.sem("x_in")
        ada_in = [m.sem(f"ada_in{i}") for i in range(3)]
        c_act, c_t, c_ts = m.sem("c_act"), m.sem("c_t"), m.sem("c_ts")
        v_t, v_ts = m.sem("v_t"), m.sem("v_ts")
        ada_used = m.sem("ada_used")
        sq_done, root_done, rstd_done, x_scaled = (m.sem(n) for n in ("sq_done", "root_done", "rstd_done", "x_scaled"))
        mod_done, amp_done, h_t, h_f, h_hi, h_lo = (m.sem(n) for n in ("mod_done", "amp_done", "h_t", "h_f", "h_hi", "h_lo"))
        m_row, m_t = m.sem("m_row"), m.sem("m_t")
        gate_out, eps_set, x_pad = m.sem("gate_out"), m.sem("eps_set"), m.sem("x_pad")
        block = ctx.enter_context(nc.Block())
        wv = A["w_ada"][0].rearrange("(k p) n -> p k n", p=P)
        NBLK = 3 * D // BC
        NCOL = 2 * D // BC

        @block.sync
        def _(sp):
            sp.dma_start(crow[0:1, :], A["c_prompt"]).then_inc(c_in, 16)
            sp.dma_start(crow[1:NSEQ, :], A["c_sample"]).then_inc(c_in, 16)
            sp.dma_start(per["ident"][:, :], A["ident"]).then_inc(c_in, 16)
            r = 0
            for name in ("b_ada", "g_pre", "g_ssm", "conv_b"):
                src = A[name].rearrange("a (r p) -> (a r) p", p=P)
                sp.dma_start(vrows[r:r + src.shape[0], :], src).then_inc(v_in, 16)
                r += src.shape[0]
            sp.dma_start(cwrows[:, :], A["conv_w"].rearrange("a k (r p) -> (a k r) p", p=P)).then_inc(v_in, 16)
            sp.dma_start(bgate[:, :], A["b_ada"][0:1, 2 * D:3 * D].to_broadcast((NSEQ, D))).then_inc(v_in, 16)
            with sp.Fori(0, NBLK // 3) as i:
                for j in range(3):
                    sp.wait_ge(ada_used, i * 3 + (j + 1))
                    sp.dma_start(raw[:, j, :, :], wv[:, :, ds((i * 3 + j) * BC, BC)]).then_inc(ada_in[j], 16)
            sp.wait_ge(m_row, NBLK)
            sp.dma_start(S["gate"], grow[:, :]).then_inc(gate_out, 16)
            sp.wait_ge(gate_out, 16)

        @block.gpsimd
        def _(pool):
            nc.gpsimd.memset(eps[:, :], EPS).then_inc(eps_set, 1)
            nc.gpsimd.memset(x[:, 4, :], 0.0).then_inc(x_pad, 1)
            pool.wait_ge(x_pad, 1)
            for t in range(4):
                pool.dma_start(x[:, t, :], A["x_prompt"][0, t * P:(t + 1) * P, :]).then_inc(x_in, 16)
            pool.dma_start(x[0:SAMP, 4, :], A["x_sample"].rearrange("b t d -> (b t) d")).then_inc(x_in, 16)

        @block.scalar
        def _(act):
            act.wait_ge(c_in, 48)
            nc.scalar.activation(cact[:, :], crow[:, :], ACT.Silu).then_inc(c_act, 1)
            act.wait_ge(x_in, 80)
            act.wait_ge(c_t, 1)
            for t in range(5):
                if t:
                    act.wait_ge(sq_done, t)
                nc.scalar.activation(sq[:, :], x[:, t, :], ACT.Square, accum_out=ssq[:, t:t + 1]).then_inc(sq_done, 1)
            act.wait_ge(sq_done, 5)
            act.wait_ge(eps_set, 1)
            nc.scalar.activation(root[:, :], ssq[:, :], ACT.Sqrt, bias=eps[:, :], scale=1.0 / D).then_inc(root_done, 1)
            for k in range(KT):
                act.wait_ge(h_f, k + 1)
                nc.scalar.activation(per["hH"][:, k, :], hF[:, k % 2, :], ACT.Copy).then_inc(h_hi, 1)

        @block.tensor
        def _(pe):
            pe.wait_ge(c_act, 1)
            pe.wait_ge(c_in, 48)
            for k in range(KT):
                mm = nc.tensor.transpose(ps_c[:, k * NSEQ:(k + 1) * NSEQ], cact[:, k * P:(k + 1) * P],
                                         per["ident"][0:NSEQ, 0:NSEQ])
            mm.then_inc(c_t, 1)
            pe.wait_ge(v_in, 96)
            nc.tensor.transpose(ps_v[:, 0:112], vrows[:, :], per["ident"][0:112, 0:112])
            nc.tensor.transpose(ps_v[:, 128:256], cwrows[:, :], per["ident"][:, :]).then_inc(v_t, 1)
            pe.wait_ge(c_ts, 1)
            pe.sem_inc(ada_used, 3)
            def columns(n):
                pe.wait_ge(m_row, n + 1)
                for c in range(2):
                    mm = nc.tensor.transpose(ps_c[:, (2 * n + c) * NSEQ:(2 * n + c + 1) * NSEQ],
                                             mrow[:, n % 2, c * P:(c + 1) * P], per["ident"][0:NSEQ, 0:NSEQ])
                mm.then_inc(m_t, 1)

            for n in range(NBLK):
                pe.wait_ge(ada_in[n % 3], 16 * (n // 3 + 1))
                if n >= 2:
                    pe.wait_ge(m_row, n - 1)
                for k in range(KT):
                    mm = nc.tensor.matmul(ps_m[n % 2][0:NSEQ, 0:BC], cT[:, k, :], raw[:, n % 3, k, :],
                                          start=(k == 0), stop=(k == KT - 1))
                mm.then_inc(ada_used, 1)
                if 1 <= n <= NCOL:
                    columns(n - 1)
            pe.wait_ge(x_scaled, 5)
            for k in range(KT):
                if k >= 2:
                    pe.wait_ge(h_f, k - 1)
                for t in range(5):
                    n = P if t < 4 else SAMP
                    mm = nc.tensor.transpose(ps_h[k % 2][:, t * P:t * P + n], x[0:n, t, k * P:(k + 1) * P],
                                             per["ident"][0:n, 0:n])
                mm.then_inc(h_t, 1)

        @block.vector
        def _(dve):
            dve.wait_ge(c_t, 1)
            nc.vector.tensor_copy(cT[:, :, :], ps_c[:, 0:KT * NSEQ].rearrange("p (k s) -> p k s", s=NSEQ)).then_inc(c_ts, 1)
            dve.wait_ge(v_t, 1)
            nc.vector.tensor_copy(per["vec"][:, 0:112], ps_v[:, 0:112]).then_inc(v_ts, 1)
            nc.vector.tensor_copy(per["vec"][:, 112:240], ps_v[:, 128:256]).then_inc(v_ts, 1)
            dve.wait_ge(root_done, 1)
            nc.vector.reciprocal(rstd[:, :], root[:, :]).then_inc(rstd_done, 1)
            dve.wait_ge(rstd_done, 1)
            for t in range(5):
                nc.vector.tensor_scalar(x[:, t, :], x[:, t, :], rstd[:, t:t + 1], None, ALU.mult).then_inc(x_scaled, 1)
            vec = per["vec"]
            for n in range(NBLK):
                dve.wait_ge(ada_used, n + 4)
                if n < NCOL:
                    if n >= 2:
                        dve.wait_ge(m_t, n - 1)
                    nc.vector.tensor_copy(mrow[:, n % 2, :], ps_m[n % 2][0:NSEQ, 0:BC]).then_inc(m_row, 1)
                else:
                    x0 = (n - NCOL) * BC
                    dve.wait_ge(v_in, 96)
                    nc.vector.tensor_tensor(grow[:, x0:x0 + BC], ps_m[n % 2][0:NSEQ, 0:BC], bgate[:, x0:x0 + BC],
                                            ALU.add).then_inc(m_row, 1)
                if n == NCOL:
                    dve.wait_ge(m_t, NCOL)
                    dve.wait_ge(v_ts, 2)
                    nc.vector.tensor_tensor(mod[:, :, :], ps_c[:, 0:2 * KT * NSEQ].rearrange("p (k s) -> p k s", s=NSEQ),
                                            vec[:, 0:2 * KT].unsqueeze(2).broadcast_to((P, 2 * KT, NSEQ)),
                                            ALU.add).then_inc(mod_done, 1)
            dve.wait_ge(mod_done, 1)
            nc.vector.scalar_tensor_tensor(amp[:, :, :], mod[:, 16:32, :], 1.0,
                                           vec[:, 48:64].unsqueeze(2).broadcast_to((P, KT, NSEQ)),
                                           ALU.add, ALU.mult).then_inc(amp_done, 1)
            dve.wait_ge(amp_done, 1)
            for k in range(KT):
                dve.wait_ge(h_t, k + 1)
                if k >= 2:
                    dve.wait_ge(h_hi, k - 1)
                    dve.wait_ge(h_lo, k - 1)
                hs = hF[:, k % 2, SEQ:TOK].rearrange("p (b t) -> p b t", t=NT)
                psm = ps_h[k % 2][:, SEQ:TOK].rearrange("p (b t) -> p b t", t=NT)
                nc.vector.tensor_tensor(hs, psm, amp[:, k, 1:NSEQ].unsqueeze(2).broadcast_to((P, NB, NT)),
                                        ALU.mult).then_inc(amp_done, 1)
                dve.wait_ge(amp_done, k + 2)
                nc.vector.tensor_tensor(hs, hs, mod[:, k, 1:NSEQ].unsqueeze(2).broadcast_to((P, NB, NT)), ALU.add)
                nc.vector.tensor_scalar(hF[:, k % 2, 0:SEQ], ps_h[k % 2][:, 0:SEQ], amp[:, k, 0:1], mod[:, k, 0:1],
                                        ALU.mult, ALU.add).then_inc(h_f, 1)
                dve.wait_ge(h_hi, k + 1)
                nc.vector.tensor_tensor(per["hL"][:, k, :], hF[:, k % 2, :], per["hH"][:, k, :].bitcast(F32),
                                        ALU.subtract).then_inc(h_lo, 1)



class Gemm:

    def __init__(self, nc, m, kt, tag):
        self.nc, self.kt = nc, kt
        self.raw = m.sb(f"w_raw{tag}", [P, 3, kt, BC])
        self.wh = m.sb(f"w_hi{tag}", [P, 2, kt, P], F32R)
        self.wl = m.sb(f"w_lo{tag}", [P, 2, kt, P], F32R)
        self.ev = m.sb(f"ev{tag}", [P, 2, TOK])
        self.acc = [m.ps(f"acc{tag}{i}", (P, 2, 512)) for i in range(2)]
        self.w_in = [m.sem(f"w_in{tag}{i}") for i in range(3)]
        self.hi = m.sem(f"hi_done{tag}")
        self.lo = m.sem(f"lo_done{tag}")
        self.used = m.sem(f"mm_done{tag}")
        self.evac = m.sem(f"evac_done{tag}")
        self.stored = [m.sem(f"stored{tag}{i}") for i in range(2)]

    def load(self, sp, n, slot, src):
        sp.wait_ge(self.lo, n * 2 + 2)
        sp.dma_start(self.raw[:, slot, 0:src.shape[1], 0:src.shape[2]], src).then_inc(self.w_in[slot], 16)

    def high(self, act, slot, uses, c, u, cols=P):
        if c == 0:
            act.wait_ge(self.w_in[slot], uses * 16 + 16)
        act.wait_ge(self.used, u + 1)
        self.nc.scalar.activation(self.wh[:, c, :, 0:cols], self.raw[:, slot, :, c * P:c * P + cols],
                                  ACT.Copy).then_inc(self.hi, 1)

    def low(self, pool, slot, c, u, cols=P):
        pool.wait_ge(self.hi, u + 1)
        self.nc.gpsimd.tensor_tensor(self.wl[:, c, :, 0:cols], self.raw[:, slot, :, c * P:c * P + cols],
                                     self.wh[:, c, :, 0:cols].bitcast(F32), ALU.subtract).then_inc(self.lo, 1)

    def multiply(self, pe, c, u, aH, aL, half, cols=P):
        if half == 0:
            pe.wait_ge(self.lo, u + 7)
            pe.wait_ge(self.evac, u + 1)
        out = self.acc[c][0:cols, half, 0:HALF]
        sl = slice(half * HALF, (half + 1) * HALF)
        kt = self.kt
        for k in range(kt):
            self.nc.tensor.matmul(out, self.wh[:, c, k, 0:cols], aH[:, k, sl], start=(k == 0), stop=False)
            self.nc.tensor.matmul(out, self.wh[:, c, k, 0:cols], aL[:, k, sl], start=False, stop=False)
            mm = self.nc.tensor.matmul(out, self.wl[:, c, k, 0:cols], aH[:, k, sl], start=False, stop=(k == kt - 1))
        if half == 1:
            mm.then_inc(self.used, 1)

    def copy_out(self, act, c, u, half_u, cols=P):
        act.wait_ge(self.stored[c], half_u * 16)
        act.wait_ge(self.used, u + 3)
        self.nc.scalar.activation(self.ev[0:cols, c, :].rearrange("p (a n) -> p a n", a=2),
                                  self.acc[c][0:cols, :, 0:HALF], ACT.Copy).then_inc(self.evac, 1)
        act.wait_ge(self.evac, u + 3)



NQB, NKVB, NRESTB, NXB, NRB = 12, 24, 5, 24, 15
B_KV = NQB
B_REST = B_KV + NKVB
B_X = B_REST + NRESTB
B_R = B_X + NXB
B_TAIL = B_R + NRB
TAIL = INW - B_TAIL * BC


def phase_proj(nc, A, S, per):
    with ExitStack() as ctx:
        m = Mem(nc, ctx)
        g = Gemm(nc, m, KT, "1")
        work = m.sb("work", [P, 4992])
        tokst = work[:, 0:1280].rearrange("p (a t e) -> p a t e", a=2, t=5)
        prod = work[:, 1280:2304]
        PTn = work[0:SAMP, 2304:3840].rearrange("p (h g t) -> p h g t", h=H, g=3)
        srow = work[0:SAMP, 3840:4416]
        msamp = work[0:SAMP, 4416:4992]
        qk = work[:, 0:3072].rearrange("p (x t) -> p x t", x=6)
        prow = work[:, 3072:3840]
        pT = work[:, 3840:4608].rearrange("p (x q) -> p x q", x=6)
        oN = work[:, 4608:4736]
        ring = m.sb("kv_ring", [P, 4 * AW])
        vP = ring[:, 2048:3584].rearrange("p (x e) -> p x e", x=12)
        za = ring[:, 3584:4096]
        oa = m.sb("oa", [P, SEQ])
        mprompt = m.sb("mprompt", [P, MASK0 + 2 * P])
        ST = m.sb("ST", [P, 3, H, SAMP])
        stat = m.sb("stat", [P, 4])
        PTb = work[:, 4736:4928].rearrange("p (g h t) -> p g h t", g=3, h=H)
        oS = per["oS"]
        qs = ring[:, 0:1536].rearrange("p (h g t) -> p h g t", h=H, g=3)
        ks = ring[:, 1536:3072].rearrange("p (h g t) -> p h g t", h=H, g=3)
        vs = ring[0:SAMP, 3072:3840].rearrange("p (a g e) -> p a g e", a=2, g=3)
        zs = ring[:, 0:512].rearrange("p (h t) -> p h t", h=H)
        ps_t = m.ps("ps_t")
        ps_w = m.ps("ps_w")
        ps_s = m.ps("ps_s", (P, 1024))

        tok_t, tok_c = m.sem("tok_t"), m.sem("tok_c")
        tok_out = [m.sem(f"tok_out{i}") for i in range(2)]
        k_in = [m.sem(f"k_in{i}") for i in range(2)]
        q_in = [m.sem(f"q_in{i}") for i in range(2)]
        v_in = [m.sem(f"v_in1{i}") for i in range(2)]
        vs_in = [m.sem(f"vs_in{i}") for i in range(2)]
        prod_done, sc_done, heads_in, mask_in, v_used, pt_b, w_read = (
            m.sem(n) for n in ("prod_done", "sc_done", "heads_in", "mask_in", "v_used", "pt_b", "w_read"))
        row_t, row_m, row_x, row_e, row_i, row_p, pt_t, pt_c, on_d, on_c = (
            m.sem(n) for n in ("row_t", "row_m", "row_x", "row_e", "row_i", "row_p", "pt_t", "pt_c", "on_d", "on_c"))
        qk_in, va_in, za_in, za_s, oa_out = (m.sem(n) for n in ("qk_in", "va_in", "za_in", "za_s", "oa_out"))
        at_sc, at_m, at_x, at_e, at_i, at_pt, at_pc, at_o, at_on, at_ot, at_g = (
            m.sem(n) for n in ("at_sc", "at_m", "at_x", "at_e", "at_i", "at_pt", "at_pc", "at_o", "at_on", "at_ot", "at_g"))
        zs_in, zs_s, os_g, os_out = (m.sem(n) for n in ("zs_in", "zs_s", "os_g", "os_out"))
        copied, dt_out, zeroed = m.sem("copied"), m.sem("dt_out"), m.sem("zeroed")
        block = ctx.enter_context(nc.Block())
        wv = A["w_in"][0].rearrange("(k p) n -> p k n", p=P)
        cache = [A["cache_a_w128"][0], A["cache_a_w512"][0], A["cache_a_w2048"][0]]
        newbuf = [A["s_kv128"][0], A["s_kv512"][0], A["s_kv2048"][0]]
        before = [sum(len(q) for _, _, q in SETS[:s]) for s in range(NSETS + 1)]

        @block.sync
        def _(sp):
            sp.dma_start(msamp, A["mask_samp"]).then_inc(mask_in, 16)
            sp.dma_start(mprompt[:, :], A["mask_prompt"]).then_inc(mask_in, 16)

            def weights(i, j, n0):
                g.load(sp, i * 3 + (n0 + j), (n0 + j) % 3, wv[:, :, ds((i * 3 + (n0 + j)) * BC, BC)])

            with sp.Fori(0, NQB // 3) as i:
                for j in range(3):
                    weights(i, j, 0)
            for j in range(2):
                weights(0, j, B_KV)
            sp.wait_ge(tok_out[0], 32 * (NQB + 1))
            sp.wait_ge(tok_out[1], 32 * NQB)
            with sp.Fori(0, NB) as b:
                nq = 0
                for s, (gi, cls, queries) in enumerate(SETS):
                    if s in (0, 8, 12):
                        weights(b, (0, 8, 12).index(s), B_KV + 2)
                    d = GROUPS[gi][1]
                    if s >= 2:
                        sp.wait_ge(prod_done, b * NQ + (before[s - 1] + NQ))
                    else:
                        sp.wait_ge(prod_done, b * NQ + before[NSETS - s])
                    sp.dma_start(ring[:, (s % 2) * AW:(s % 2 + 1) * AW],
                                 cache[gi][ds(b, 1), cls:cls + (P - 1) * d + 1:d, 0, :, :].rearrange("b s h e -> s (b h e)")
                                 ).then_inc(k_in[s % 2], 16)
                    for t in queries:
                        sp.wait_ge(prod_done, b * NQ + (nq - 1 + NQ))
                        sp.dma_start(ring[:, (2 + nq % 2) * AW:(3 + nq % 2) * AW],
                                     S["kvtok"][ds(b * NT + (SEQ + t), 1), P + gi * AW:P + (gi + 1) * AW].to_broadcast((P, AW))
                                     ).then_inc(q_in[nq % 2], 16)
                        nq += 1
            weights(0, 2, B_REST)
            sp.wait_ge(prod_done, NB * NQ + NQ)
            for c in range(2):
                sp.wait_ge(g.stored[c], 16 * B_REST)
            for dst, w in ((qs, 0), (ks, 1)):
                for gi in range(3):
                    sp.dma_start(dst[:, :, gi, :],
                                 S["projT"][w * QKV + gi * AW:w * QKV + (gi + 1) * AW, SEQ:TOK].rearrange("(h e) t -> e h t", h=H)
                                 ).then_inc(heads_in, 16)
            sp.wait_ge(tok_out[0], 32 * (B_REST + 1))
            sp.wait_ge(tok_out[1], 32 * B_REST)
            for h in range(H):
                if h >= 2:
                    sp.wait_ge(on_d, h - 1)
                sp.dma_start(vs[:, h % 2, :, :],
                             S["kvtok"][SEQ:TOK, P + 2 * QKV:P + 3 * QKV].rearrange("t (g h e) -> h t g e", g=3, h=H)[h]
                             ).then_inc(vs_in[h % 2], 16)
                if h in (2, 4, 6, 7):
                    weights(0, 3 + (2, 4, 6, 7).index(h), B_REST)
            sp.wait_ge(on_d, H)
            qkT = S["projT"][0:2 * QKV, 0:SEQ].rearrange("(x h e) t -> h e x t", x=6, h=H)
            with sp.Fori(0, NB) as b:
                for s, (gi, cls, queries) in enumerate(reversed(SETS)):
                    if s in (2, 5, 8):
                        weights(b, (2, 5, 8).index(s), B_X + 2)
                    d = GROUPS[gi][1]
                    if s < 2:
                        sp.wait_ge(v_used, b * NSETS + (NSETS - s))
                    else:
                        sp.wait_ge(v_used, b * NSETS + (s - 1 + NSETS))
                    sp.dma_start(ring[:, (s % 2) * AW:(s % 2 + 1) * AW],
                                 cache[gi][ds(b, 1), cls:cls + (P - 1) * d + 1:d, 1, :, :].rearrange("b s h e -> s (b h e)")
                                 ).then_inc(v_in[s % 2], 16)
                    if s == 0:
                        sp.wait_ge(at_sc, b * 4)
                        sp.dma_start(qk[:, :, :], qkT[ds(b, 1)].rearrange("a e x t -> e (a x) t")).then_inc(qk_in, 16)
                        sp.wait_ge(at_g, b * 4)
                        sp.dma_start(za, S["projT"][ds(b * E + COL_ZA, E), 0:SEQ]).then_inc(za_in, 16)
                        for gi2 in range(3):
                            rows = S["kvtok"][0:SEQ, ds(b * E + (P + 2 * QKV + gi2 * AW), E)]
                            order = "(x p) n -> p x n" if gi2 == 0 else "(p x) n -> p x n"
                            sp.dma_start(vP[:, 4 * gi2:4 * gi2 + 4, :], rows.rearrange(order, x=4)).then_inc(va_in, 16)
            sp.wait_ge(v_used, (NB + 1) * NSETS)
            sp.dma_start(zs, S["projT"][COL_ZA:COL_ZA + AW, SEQ:TOK].rearrange("(h e) t -> e h t", h=H)).then_inc(zs_in, 16)
            with sp.Fori(0, 4) as i:
                for j in range(3):
                    weights(i, j, B_R + 2)
            weights(0, 14, B_R)
            g.load(sp, B_TAIL, B_TAIL % 3, wv[:, :, B_TAIL * BC:INW])
            sp.wait_ge(os_g, 1)
            sp.dma_start(S["oaT"][:, SEQ:TOK].rearrange("(h e) t -> e h t", h=H), per["oS"][:, :, :]).then_inc(os_out, 16)
            sp.wait_ge(os_out, 16)

        @block.gpsimd
        def _(pool):
            pool.sem_inc(g.lo, 6)
            nc.gpsimd.memset(g.ev[:, 1, :], 0.0).then_inc(zeroed, 1)

            pieces = [(2, 204 * x, 204) for x in range(10)] + [(1, 168 * x, 168) for x in range(3)] + [(0, 0, 120)]

            def copy(b, piece):
                gi, row, n = piece
                src = cache[gi][ds(b, 1), NT + row:NT + row + n, :, :, :].rearrange("b s k h e -> (b s k h e)")
                dst = newbuf[gi][ds(b, 1), row:row + n, :, :, :].rearrange("b s k h e -> (b s k h e)")
                pool.dma_start(dst.rearrange("(q x) -> q x", q=16), src.rearrange("(q x) -> q x", q=16)).then_inc(copied, 16)

            def lows(i, n0, blocks=3, per_it=6, b=None):
                units = 2 * blocks
                for x in range(units):
                    g.low(pool, (n0 + x // 2) % 3, x % 2, i * per_it + (2 * n0 + x))
                    if b is not None:
                        for piece in pieces[len(pieces) * x // units:len(pieces) * (x + 1) // units]:
                            copy(b, piece)

            with pool.Fori(0, NQB // 3) as i:
                lows(i, 0, b=i)
            with pool.Fori(0, NKVB // 3) as i:
                lows(i, B_KV)
            lows(0, B_REST, NRESTB)
            with pool.Fori(0, NXB // 6) as i:
                lows(i, B_X, 6, 12, b=i + NQB // 3)
            with pool.Fori(0, NRB // 3) as i:
                lows(i, B_R)
            g.low(pool, B_TAIL % 3, 0, 2 * B_TAIL, TAIL)
            pool.wait_ge(copied, 16 * len(pieces) * NB)

        @block.scalar
        def _(act):
            act.sem_inc(g.evac, 2)

            def split_next(i, x, n0, per_it, cols=P):
                u = i * (2 * per_it) + (2 * n0 + x)
                nb = n0 + (x + 1) // 2
                g.high(act, nb % 3, (i if per_it else 0) + nb // 3, (x + 1) % 2, u + 1, cols)

            def store_rows(i, x, n0, per_it):
                u, c = i * (2 * per_it) + (2 * n0 + x), x % 2
                act.wait_ge(tok_t, u + 1)
                act.wait_ge(tok_out[c], i * (32 * per_it) + 32 * (n0 + x // 2))
                nc.scalar.activation(tokst[:, c, 0:4, :], ps_t[:, :].rearrange("p (t e) -> p t e", e=P),
                                     ACT.Copy).then_inc(tok_c, 1)
                nc.scalar.activation(tokst[0:SAMP, c, 4, :], ps_w[0:SAMP, 0:P], ACT.Copy).then_inc(tok_c, 1)
                act.wait_ge(tok_c, u * 2 + 2)
                dst = S["kvtok"][:, ds(u * P, P)]
                act.dma_start(dst[0:SEQ, :].rearrange("(t p) n -> p t n", p=P), tokst[:, c, 0:4, :]).then_inc(tok_out[c], 16)
                act.dma_start(dst[SEQ:TOK, :], tokst[0:SAMP, c, 4, :]).then_inc(tok_out[c], 16)

            def store_unit(i, x, n0, per_it):
                u, c = i * (2 * per_it) + (2 * n0 + x), x % 2
                g.copy_out(act, c, u, i * per_it + (n0 + x // 2))
                act.dma_start(S["projT"][ds(u * P, P), :], g.ev[:, c, :]).then_inc(g.stored[c], 16)

            act.wait_ge(zeroed, 1)
            g.high(act, 0, 0, 0, 0)
            for n0, blocks in ((0, NQB), (B_KV, NKVB)):
                with act.Fori(0, blocks // 3) as i:
                    for x in range(6):
                        split_next(i, x, n0, 3)
                        store_rows(i, x, n0, 3)
                        store_unit(i, x, n0, 3)
            for x in range(2 * NRESTB):
                split_next(0, x, B_REST, 0)
                if x == 0:
                    store_rows(0, x, B_REST, 0)
                store_unit(0, x, B_REST, 0)
                if x < H:
                    act.wait_ge(row_x, x + 1)
                    nc.scalar.activation(srow, srow, ACT.Exp, bias=stat[0:SAMP, 1:2], scale=SCALE,
                                         accum_out=stat[0:SAMP, 2:3]).then_inc(row_e, 1)

            def attention(b, x):
                r = x // 3
                if x == 0:
                    act.wait_ge(za_in, b * 16 + 16)
                    nc.scalar.activation(za, za, ACT.Silu).then_inc(za_s, 1)
                if x % 3 == 0:
                    act.wait_ge(at_x, b * 4 + (r + 1))
                    nc.scalar.activation(prow, prow, ACT.Exp, bias=stat[:, 1:2], scale=SCALE,
                                         accum_out=stat[:, 2:3]).then_inc(at_e, 1)
                if x % 3 == 1:
                    act.wait_ge(at_pt, b * 4 + (r + 1))
                    act.wait_ge(at_o, b * 4 + r)
                    nc.scalar.activation(pT[:, :, :], ps_s[:, 0:768].rearrange("p (x q) -> p x q", x=6),
                                         ACT.Copy).then_inc(at_pc, 1)

            with act.Fori(0, NB) as b:
                for x in range(6):
                    split_next(b, x, B_X, 3)
                    attention(b, 2 * x)
                    store_unit(b, x, B_X, 3)
                    attention(b, 2 * x + 1)
                act.wait_ge(at_g, b * 4 + 4)
                act.dma_start(S["oaT"][ds(b * E, E), 0:SEQ], oa[:, :]).then_inc(oa_out, 16)
            act.wait_ge(zs_in, 16)
            nc.scalar.activation(zs, zs, ACT.Silu).then_inc(zs_s, 1)
            with act.Fori(0, NRB // 3 - 1) as i:
                for x in range(6):
                    split_next(i, x, B_R, 3)
                    store_unit(i, x, B_R, 3)
            i = NRB // 3 - 1
            for x in range(6):
                split_next(i, x, B_R, 3, TAIL if x == 5 else P)
                store_unit(i, x, B_R, 3)
            g.copy_out(act, 0, 2 * B_TAIL, B_TAIL, TAIL)
            act.dma_start(S["projT"][B_TAIL * BC:INW, :], g.ev[0:TAIL, 0, :]).then_inc(g.stored[0], 16)
            act.wait_ge(g.stored[0], 16 * (B_TAIL + 1))
            act.wait_ge(g.stored[1], 16 * B_TAIL)
            act.wait_ge(oa_out, 16 * H)

        @block.tensor
        def _(pe):
            pe.sem_inc(g.used, 2)
            hH, hL, ident = per["hH"], per["hL"], per["ident"]

            def token_rows(c, u):
                pe.wait_ge(g.evac, u + 2)
                pe.wait_ge(tok_c, u * 2)
                for t in range(4):
                    nc.tensor.transpose(ps_t[:, t * P:(t + 1) * P], g.ev[:, 1 - c, t * P:(t + 1) * P], ident[:, :])
                nc.tensor.transpose(ps_w[0:SAMP, 0:P], g.ev[:, 1 - c, SEQ:TOK], ident[:, :]).then_inc(tok_t, 1)

            pe.wait_ge(zeroed, 1)
            for n0, blocks in ((0, NQB), (B_KV, NKVB)):
                with pe.Fori(0, blocks // 3) as i:
                    for x in range(6):
                        u = i * 6 + (2 * n0 + x)
                        g.multiply(pe, x % 2, u, hH, hL, 0)
                        token_rows(x % 2, u)
                        g.multiply(pe, x % 2, u, hH, hL, 1)

            def head_scores(h):
                if h == 0:
                    pe.wait_ge(sc_done, NB * NQ)
                    pe.wait_ge(heads_in, 96)
                else:
                    pe.wait_ge(pt_c, 2 * h)
                for gi in range(3):
                    nc.tensor.transpose(ps_s[0:SAMP, gi * P:(gi + 1) * P], ST[:, gi, h, :], ident[:, :])
                for gi in range(3):
                    mm = nc.tensor.matmul(ps_s[0:SAMP, 512 + gi * SAMP:512 + (gi + 1) * SAMP], qs[:, h, gi, :],
                                          ks[:, h, gi, :], start=True, stop=True)
                mm.then_inc(row_t, 1)

            def head_values(h):
                pe.wait_ge(row_p, h + 1)
                for gi in range(3):
                    nc.tensor.transpose(ps_s[:, gi * SAMP:(gi + 1) * SAMP], srow[:, gi * P:(gi + 1) * P],
                                        ident[0:SAMP, 0:SAMP])
                for gi in range(3):
                    mm = nc.tensor.transpose(ps_s[0:SAMP, 512 + gi * SAMP:512 + (gi + 1) * SAMP],
                                             srow[:, 384 + gi * SAMP:384 + (gi + 1) * SAMP], ident[0:SAMP, 0:SAMP])
                mm.then_inc(pt_t, 1)

            def head_new(h):
                pe.wait_ge(pt_c, 2 * h + 2)
                pe.wait_ge(vs_in[h % 2], 16 * (h // 2 + 1))
                if h == 0:
                    pe.wait_ge(tok_c, 2 * (2 * B_REST + 1))
                for gi in range(3):
                    mm = nc.tensor.matmul(ps_w[:, h * SAMP:(h + 1) * SAMP], vs[:, h % 2, gi, :], PTn[:, h, gi, :],
                                          start=(gi == 0), stop=(gi == 2))
                mm.then_inc(on_d, 1)

            for x in range(2 * NRESTB):
                u = 2 * B_REST + x
                g.multiply(pe, x % 2, u, hH, hL, 0)
                if x == 0:
                    token_rows(0, u)
                elif x <= H:
                    head_values(x - 1)
                g.multiply(pe, x % 2, u, hH, hL, 1)
                if 1 <= x <= H:
                    head_new(x - 1)
                if x < H:
                    head_scores(x)

            def value_set(b, s):
                gi, cls, queries = SETS[NSETS - 1 - s]
                if s == 0:
                    pe.wait_ge(pt_b, b + 1)
                pe.wait_ge(v_in[s % 2], b * (16 * (7, 6)[s % 2]) + 16 * (s // 2 + 1))
                step = queries[1] - queries[0] if len(queries) > 1 else 1
                sl = slice(queries[0], queries[-1] + 1, step)
                for h in range(H):
                    mm = nc.tensor.matmul(
                        ps_w[:, h * NT:(h + 1) * NT][:, sl],
                        ring[:, (s % 2) * AW + h * E:(s % 2) * AW + (h + 1) * E], PTb[:, gi, h, sl],
                        start=(s == 0 and h == 0), stop=(s == NSETS - 1 and h == H - 1),
                        skip_group_check=True)
                mm.then_inc(v_used, 1)

            def rows_back(b, r):
                pe.wait_ge(at_on, b * 4 + (r + 1))
                nc.tensor.transpose(ps_t[:, P:2 * P], oN, ident[:, :]).then_inc(at_ot, 1)

            def attention(b, x):
                r = x // 3
                if x % 3 == 0:
                    if r:
                        rows_back(b, r - 1)
                    if r == 0:
                        pe.wait_ge(qk_in, b * 16 + 16)
                    pe.wait_ge(at_pc, b * 4 + r)
                    nc.tensor.matmul(ps_s[:, 0:512], qk[:, 0, r:SEQ:4], qk[:, 3, :], start=True, stop=True)
                    nc.tensor.matmul(ps_s[:, 512:640], qk[:, 1, r:SEQ:4], qk[:, 4, r:SEQ:4], start=True, stop=True)
                    nc.tensor.matmul(ps_s[:, 640:768], qk[:, 2, r:SEQ:4], qk[:, 5, r:SEQ:4], start=True,
                                     stop=True).then_inc(at_sc, 1)
                elif x % 3 == 1:
                    pe.wait_ge(at_e, b * 4 + (r + 1))
                    for y in range(6):
                        mm = nc.tensor.transpose(ps_s[:, y * P:(y + 1) * P], prow[:, y * P:(y + 1) * P], ident[:, :])
                    mm.then_inc(at_pt, 1)
                else:
                    pe.wait_ge(at_pc, b * 4 + (r + 1))
                    if r == 0:
                        pe.wait_ge(va_in, b * 48 + 48)
                    for y in range(6):
                        vt = y if y < 4 else (4 + r if y == 4 else 8 + r)
                        mm = nc.tensor.matmul(ps_t[:, 0:P], pT[:, y, :], vP[:, vt, :], start=(y == 0), stop=(y == 5))
                    mm.then_inc(at_o, 1)

            with pe.Fori(0, NB) as b:
                s = 0
                for x in range(12):
                    u = b * 6 + (2 * B_X + x // 2)
                    g.multiply(pe, (x // 2) % 2, u, hH, hL, x % 2)
                    attention(b, x)
                    for _ in range(2 if x == 0 else 1):
                        value_set(b, s)
                        s += 1
                rows_back(b, 3)
                assert s == NSETS
            with pe.Fori(0, NRB // 3) as i:
                for x in range(6):
                    for half in range(2):
                        g.multiply(pe, x % 2, i * 6 + (2 * B_R + x), hH, hL, half)
            for half in range(2):
                g.multiply(pe, 0, 2 * B_TAIL, hH, hL, half, TAIL)

        @block.vector
        def _(dve):
            dve.sem_inc(prod_done, NQ)
            dve.sem_inc(v_used, NSETS)
            with dve.Fori(0, NB) as b:
                nq = 0
                for s, (gi, cls, queries) in enumerate(SETS):
                    kuses = (7, 6)[s % 2]
                    dve.wait_ge(k_in[s % 2], b * (16 * kuses) + 16 * (s // 2 + 1))
                    for t in queries:
                        dve.wait_ge(q_in[nq % 2], b * (8 * NQ) + 16 * (nq // 2 + 1))
                        dve.wait_ge(sc_done, b * NQ + nq)
                        nc.vector.tensor_tensor(prod, ring[:, (s % 2) * AW:(s % 2 + 1) * AW],
                                                ring[:, (2 + nq % 2) * AW:(3 + nq % 2) * AW], ALU.mult).then_inc(prod_done, 1)
                        dve.wait_ge(prod_done, b * NQ + (nq + 1 + NQ))
                        nc.vector.tensor_reduce(ST[:, gi, :, ds(b * NT + t, 1)],
                                                prod.rearrange("p (h e) -> p h e", e=E), AX, ALU.add).then_inc(sc_done, 1)
                        nq += 1
            dve.wait_ge(mask_in, 32)
            for h in range(H):
                dve.wait_ge(row_t, h + 1)
                if h:
                    dve.wait_ge(pt_t, h)
                nc.vector.tensor_tensor(srow[:, 0:384], ps_s[0:SAMP, 0:384], msamp[:, 0:384], ALU.add).then_inc(row_m, 1)
                nc.vector.tensor_tensor(srow[:, 384:576], ps_s[0:SAMP, 512:704], msamp[:, 384:576], ALU.add).then_inc(row_m, 1)
                dve.wait_ge(row_m, 3 * h + 2)
                nc.vector.reduce_max(stat[0:SAMP, 0:1], srow, AX).then_inc(row_m, 1)
                dve.wait_ge(row_m, 3 * h + 3)
                nc.vector.tensor_scalar(stat[0:SAMP, 1:2], stat[0:SAMP, 0:1], -SCALE, None, ALU.mult).then_inc(row_x, 1)
                dve.wait_ge(row_e, h + 1)
                nc.vector.reciprocal(stat[0:SAMP, 3:4], stat[0:SAMP, 2:3]).then_inc(row_i, 1)
                dve.wait_ge(row_i, h + 1)
                nc.vector.tensor_scalar(srow, srow, stat[0:SAMP, 3:4], None, ALU.mult).then_inc(row_p, 1)
                dve.wait_ge(pt_t, h + 1)
                nc.vector.tensor_copy(ST[:, :, h, :], ps_s[:, 0:192].rearrange("p (g t) -> p g t", g=3)).then_inc(pt_c, 1)
                nc.vector.tensor_copy(PTn[:, h, :, :], ps_s[0:SAMP, 512:704].rearrange("p (g t) -> p g t", g=3)).then_inc(pt_c, 1)
            dve.wait_ge(on_d, H)
            nc.vector.tensor_copy(oS[:, :, :], ps_w[:, :].rearrange("p (h t) -> p h t", h=H)).then_inc(on_c, 1)
            dve.wait_ge(on_c, 1)
            dve.wait_ge(pt_c, 2 * H)

            def gate(b, r):
                dve.wait_ge(at_ot, b * 4 + (r + 1))
                if r == 0:
                    dve.wait_ge(za_s, b + 1)
                    dve.wait_ge(oa_out, b * 16)
                nc.vector.tensor_tensor(oa[:, r:SEQ:4], ps_t[:, P:2 * P], za[:, r:SEQ:4], ALU.mult).then_inc(at_g, 1)

            with dve.Fori(0, NB) as b:
                nc.vector.tensor_copy(PTb[:, :, :, :], ST[:, :, :, ds(b * NT, NT)]).then_inc(pt_b, 1)
                for r in range(4):
                    if r:
                        gate(b, r - 1)
                    dve.wait_ge(at_sc, b * 4 + (r + 1))
                    dve.wait_ge(at_pt, b * 4 + r)
                    nc.vector.tensor_tensor(prow[:, 0:SEQ], ps_s[:, 0:SEQ], mprompt[:, 3 - r:3 - r + SEQ], ALU.add).then_inc(at_m, 1)
                    nc.vector.tensor_tensor(prow[:, SEQ:768], ps_s[:, SEQ:768], mprompt[:, MASK0:MASK0 + 2 * P],
                                            ALU.add).then_inc(at_m, 1)
                    dve.wait_ge(at_m, b * 12 + (3 * r + 2))
                    nc.vector.reduce_max(stat[:, 0:1], prow, AX).then_inc(at_m, 1)
                    dve.wait_ge(at_m, b * 12 + (3 * r + 3))
                    nc.vector.tensor_scalar(stat[:, 1:2], stat[:, 0:1], -SCALE, None, ALU.mult).then_inc(at_x, 1)
                    dve.wait_ge(at_e, b * 4 + (r + 1))
                    nc.vector.reciprocal(stat[:, 3:4], stat[:, 2:3]).then_inc(at_i, 1)
                    dve.wait_ge(at_i, b * 4 + (r + 1))
                    dve.wait_ge(at_o, b * 4 + (r + 1))
                    nc.vector.tensor_scalar(oN, ps_t[:, 0:P], stat[:, 3:4], None, ALU.mult).then_inc(at_on, 1)
                dve.wait_ge(v_used, b * NSETS + 2 * NSETS)
                nc.vector.tensor_tensor(oS[:, :, ds(b * NT, NT)], oS[:, :, ds(b * NT, NT)],
                                        ps_w[:, 0:H * NT].rearrange("p (h t) -> p h t", h=H), ALU.add).then_inc(w_read, 1)
                gate(b, 3)
                dve.wait_ge(w_read, b + 1)
            dve.wait_ge(zs_s, 1)
            nc.vector.tensor_tensor(oS[:, :, :], oS[:, :, :], zs, ALU.mult).then_inc(os_g, 1)



CHUNKS = [(c, c * P, P) for c in range(4)] + [(4, SEQ, SAMP)]
CSL = slice(NT - 1, SAMP, NT)


def phase_ssm(nc, A, S, per):
    with ExitStack() as ctx:
        m = Mem(nc, ctx)
        ext = m.sb("ext", [P, 4, SEQ + 3])
        exs = m.sb("exs", [P, 4, SAMP])
        extS = m.sb("extS", [P, 4, NB, NT + 3])
        stc = m.sb("stc", [3 * NB, 4, P])
        sel = m.sb("sel", [P, 4, 27])
        selr = m.sb("selr", [27, 4 * P])
        xa = m.sb("xa", [P, 4, TOK])
        zb = m.sb("zb", [P, 2, TOK])
        csr = m.sb("csr", [P, 4, TOK])
        h0 = m.sb("h0", [P, 2, NB, P])
        h0T = m.sb("h0T", [P, 2, 4 * P])
        xdt = m.sb("xdt", [P, 5, 4, 64])
        Bt = m.sb("Bt", [P, 5, P])
        Bm = m.sb("Bm", [SAMP, NB, P])
        dec = m.sb("dec", [P, 4, P])
        El = m.sb("El", [P, 4, P])
        Cs = m.sb("Cs", [P, 4, P])
        CBm = m.sb("CBm", [P, P])
        xde = m.sb("xde", [P, 4, 64])
        de4 = m.sb("de4", [P, 4])
        lastm = m.sb("lastm", [SAMP, 4, NB])
        St = m.sb("St", [P, 4 * 64])
        Sout = m.sb("Sout", [P, 2, P])
        yT = m.sb("yT", [P, 2, TOK])
        yo = m.sb("yo", [P, 2, SAMP])
        ysq = m.sb("ysq", [P, 2, TOK])
        rst = m.sb("rst", [P, TOK])
        cwl = m.sb("cwl", [P, 5, 4])
        gvl = m.sb("gvl", [P, 2])
        dkl = m.sb("dkl", [P, 2])
        dtg = m.sb("dtg", [P, 5, 4])
        csg = m.sb("csg", [P, 5, 4])
        dr = m.sb("dr", [SH, TOK])
        dn = m.sb("dn", [SH, TOK])
        dtv = m.sb("dtv", [SH, TOK])
        csv = m.sb("csv", [SH, TOK])
        seg = m.sb("seg", [SH, TOK])
        hv = m.sb("hv", [SH, 4])
        dtt = m.sb("dtt", [P, 5, SH])
        cst = m.sb("cst", [P, 5, SH])
        dsk = m.sb("dsk", [P, KT])
        causal = m.sb("causal_sb", [P, P])
        blockm = m.sb("blockm", [SAMP, SAMP])
        owner = m.sb("owner_sb", [SAMP, NB])
        ones = m.sb("ones_m", [P, P])
        eps = m.sb("eps_s", [P, 1])
        X = [m.ps("ssm_x0"), m.ps("ssm_x1")]
        Y = m.ps("ssm_y")
        Z = m.ps("ssm_z")

        sems = {}
        per_it = {
            "ext_in": 48, "exs_in": 48, "stc_in": 48, "zb_in": 16, "csr_in": 16, "h0_in": 32,
            "loc": 12, "st_t": 1, "ext_s": 2, "sel_d": 2, "sel_t": 1, "sel_c": 1, "conv_out": 96,
            "cv": 32, "xa_s": 1, "zb_s": 1, "tt": 5, "xd": 5, "bt": 5,
            "cb_t": 5, "cb_m": 5, "dd": 20, "de": 5, "el": 5, "d4": 5, "e4": 5, "xe": 5, "md": 5, "cs": 4,
            "yt": 5, "stt": 4, "yd": 10, "sd": 8, "lm": 2, "h0_t": 4, "h0_c": 4, "ys_t": 4, "yo_d": 4, "ya": 1,
            "bm": 1, "sn_t": 4, "sn_m": 4, "sn_a": 4, "s_out": 32, "ps_t": 1, "ps_c": 1, "p_out": 32,
            "yg": 1, "sq": 1, "ss_t": 1, "rt": 2, "ri": 1, "yr": 1, "yn": 2, "y_out": 16, "s0": 1,
        }
        for name in per_it:
            sems[name] = m.sem("m_" + name)
        pre_in, pre_out, const_set = m.sem("pre_in"), m.sem("pre_out"), m.sem("const_set")
        rows_out, pe_step = m.sem("rows_out"), m.sem("pe_step")
        pre_d, pre_a, pre_t = m.sem("pre_d"), m.sem("pre_a"), m.sem("pre_t")

        def wait(eng, name, g, n):
            eng.wait_ge(sems[name], g * per_it[name] + n)

        block = ctx.enter_context(nc.Block())

        @block.sync
        def _(sp):
            sp.dma_start(dr[:, :], S["projT"][COL_DT:COL_DT + SH, :]).then_inc(pre_in, 16)
            sp.dma_start(seg[:, :], A["seg"]).then_inc(pre_in, 16)
            sp.dma_start(hv[:, 0:1], A["dt_bias"].rearrange("a h -> h a")).then_inc(pre_in, 16)
            sp.dma_start(hv[:, 1:2], A["a_log"].rearrange("a h -> h a")).then_inc(pre_in, 16)
            with nc.allow_non_contiguous_dma(reason="one value a descriptor, once"):
                for hh in range(2):
                    sp.dma_start(dsk[64 * hh:64 * hh + 64, :], A["d_skip"][0:1, hh:SH:2].to_broadcast((64, KT))).then_inc(pre_in, 16)
            sp.dma_start(causal[:, :], A["causal"]).then_inc(pre_in, 16)
            sp.dma_start(blockm[:, :], A["block"]).then_inc(pre_in, 16)
            sp.dma_start(owner[:, :], A["owner"]).then_inc(pre_in, 16)
            sp.wait_ge(pre_d, 5)
            sp.dma_start(S["csT"], csv[:, :]).then_inc(pre_out, 16)
            sp.wait_ge(pre_out, 16)
            tiles = ((0, 2, 0, 2 * P), (2, 1, D, P), (3, 1, D + SG * P, P))
            with sp.Fori(0, SG) as g:
                wait(sp, "cv", g, 0)
                for q, n, ch, step in tiles:
                    rows = S["projT"][ds(g * step + (COL_XBC + ch), n * P), :].rearrange("(q p) t -> p q t", p=P)
                    sp.dma_start(ext[:, q:q + n, 3:3 + SEQ], rows[:, :, 0:SEQ]).then_inc(sems["ext_in"], 16)
                    sp.dma_start(exs[:, q:q + n, :], rows[:, :, SEQ:TOK]).then_inc(sems["exs_in"], 16)
                    sp.dma_start(stc[:, q:q + n, :].rearrange("r q p -> r (q p)"),
                                 A["state_conv"][0].rearrange("b k c -> (b k) c")[:, ds(g * step + ch, n * P)]
                                 ).then_inc(sems["stc_in"], 16)
                wait(sp, "yg", g, 0)
                sp.dma_start(zb[:, :, :], S["projT"][ds(g * 2 * P + COL_ZB, 2 * P), :].rearrange("(q p) t -> p q t", p=P)
                             ).then_inc(sems["zb_in"], 16)
                wait(sp, "xe", g, 0)
                sp.dma_start(csr[:, :, :].rearrange("p h t -> p (h t)"),
                             S["csT"][ds(g * 4, 4), :].rearrange("h t -> (h t)").unsqueeze(0).to_broadcast((P, 4 * TOK))
                             ).then_inc(sems["csr_in"], 16)
                wait(sp, "s_out", g, 0)
                h0s = A["state_ssm"][0].rearrange("b (g j h) p n -> g j (h p) b n", g=SG, j=2)
                for j in range(2):
                    sp.dma_start(h0[:, j, :, :], h0s[ds(g, 1)][0:1, j].rearrange("a q b n -> (a q) b n")).then_inc(sems["h0_in"], 16)
            for name in ("conv_out", "s_out", "p_out", "y_out"):
                sp.wait_ge(sems[name], SG * per_it[name])

        @block.gpsimd
        def _(pool):
            nc.gpsimd.memset(ones[:, :], 1.0).then_inc(const_set, 1)
            nc.gpsimd.memset(eps[:, :], EPS).then_inc(const_set, 1)
            nc.gpsimd.memset(ext[:, :, 0:3], 0.0).then_inc(const_set, 1)
            kvt = S["kvtok"]
            for kv, c0 in ((0, P + COL_K), (1, P + COL_V)):
                for gr, (win, _) in enumerate(GROUPS):
                    first = max(SEQ - win, 0)
                    cols = slice(c0 + gr * AW, c0 + (gr + 1) * AW)
                    pool.dma_start(A[f"p_kv{win}"][0, 0, :, kv].rearrange("t h e -> t (h e)"),
                                   kvt[first:SEQ, cols]).then_inc(rows_out, 16)
                    pool.dma_start(A[f"s_kv{win}"][0, :, win - NT:win, kv].rearrange("b t h e -> b t (h e)"),
                                   kvt[SEQ:TOK, cols].rearrange("(b t) c -> b t c", t=NT)).then_inc(rows_out, 16)
            pool.wait_ge(pre_d, 9)
            cw = per["vec"][:, 112:240].rearrange("p (k c) -> p k c", k=CW)
            cb, gs = per["vec"][:, 80:112], per["vec"][:, 64:80]
            with pool.Fori(0, SG) as g:
                wait(pool, "cv", g, 0)
                wait(pool, "yn", g, 0)
                wait(pool, "yd", g, 0)
                wait(pool, "d4", g, 0)
                wait(pool, "dd", g, 0)
                wait(pool, "xd", g, 0)
                for q, n, start in ((0, 2, g * 2), (2, 1, g + 2 * SG), (3, 1, g + 3 * SG)):
                    nc.gpsimd.tensor_copy(cwl[:, 0:CW, q:q + n], cw[:, :, ds(start, n)]).then_inc(sems["loc"], 1)
                    nc.gpsimd.tensor_copy(cwl[:, CW, q:q + n], cb[:, ds(start, n)]).then_inc(sems["loc"], 1)
                nc.gpsimd.tensor_copy(gvl[:, :], gs[:, ds(g * 2, 2)]).then_inc(sems["loc"], 1)
                nc.gpsimd.tensor_copy(dkl[:, :], dsk[:, ds(g * 2, 2)]).then_inc(sems["loc"], 1)
                for dst, src in ((dtg, dtt), (csg, cst)):
                    nc.gpsimd.tensor_copy(dst[:, 0:4, :], src[:, 0:4, ds(g * 4, 4)]).then_inc(sems["loc"], 1)
                    nc.gpsimd.tensor_copy(dst[0:SAMP, 4, :], src[0:SAMP, 4, ds(g * 4, 4)]).then_inc(sems["loc"], 1)
                wait(pool, "bt", g, 5)
                wait(pool, "sn_t", g, 0)
                nc.gpsimd.tensor_tensor(Bm[:, :, :], Bt[0:SAMP, 4, :].unsqueeze(1).broadcast_to((SAMP, NB, P)),
                                        owner[:, :].unsqueeze(2).broadcast_to((SAMP, NB, P)), ALU.mult).then_inc(sems["bm"], 1)
                wait(pool, "el", g, 5)
                wait(pool, "h0_t", g, 4)
                for hh in range(2):
                    for j in range(2):
                        part = slice(64 * hh, 64 * hh + 64)
                        nc.gpsimd.tensor_tensor(h0[part, j, :, :], h0[part, j, :, :],
                                                El[part, 2 * j + hh, CSL].unsqueeze(2).broadcast_to((64, NB, P)),
                                                ALU.mult).then_inc(sems["sn_m"], 1)
            pool.wait_ge(rows_out, 12 * 16)

        @block.scalar
        def _(act):
            act.wait_ge(pre_d, 2)
            act.wait_ge(const_set, 3)
            nc.scalar.activation(dn[:, :], dn[:, :], ACT.Exp).then_inc(pre_a, 1)
            act.wait_ge(pre_a, 1)
            nc.scalar.activation(dn[:, :], dn[:, :], ACT.Ln, bias=ones[0:SH, 0:1]).then_inc(pre_a, 1)
            nc.scalar.activation(hv[:, 2:3], hv[:, 1:2], ACT.Exp).then_inc(pre_a, 1)
            with act.Fori(0, SG) as g:
                wait(act, "sel_t", g, 1)
                wait(act, "conv_out", g, 0)
                nc.scalar.activation(selr[:, :], X[1][0:27, :], ACT.Copy).then_inc(sems["sel_c"], 1)
                wait(act, "sel_c", g, 1)
                for q, n, ch, step in ((0, 2, 0, 2 * P), (2, 1, D, P), (3, 1, D + SG * P, P)):
                    for dst, rows in ((A["p_conv"][0].rearrange("b k c -> (b k) c"), slice(0, 3)),
                                      (A["s_conv"][0].rearrange("b k c -> (b k) c"), slice(3, 27))):
                        act.dma_start(dst[:, ds(g * step + ch, n * P)], selr[rows, q * P:(q + n) * P]).then_inc(sems["conv_out"], 16)
                wait(act, "cv", g, 32)
                nc.scalar.activation(xa[:, :, :], xa[:, :, :], ACT.Silu).then_inc(sems["xa_s"], 1)
                wait(act, "zb_in", g, 16)
                nc.scalar.activation(zb[:, :, :], zb[:, :, :], ACT.Silu).then_inc(sems["zb_s"], 1)
                wait(act, "stt", g, 0)
                wait(act, "bm", g, 0)
                for t, _, n in CHUNKS:
                    wait(act, "tt", g, t + 1)
                    wait(act, "xd", g, t + 1)
                    nc.scalar.activation(Bt[0:n, t, :], X[t % 2][0:n, 2 * P:3 * P], ACT.Copy).then_inc(sems["bt"], 1)
                wait(act, "csr_in", g, 16)
                wait(act, "sn_m", g, 0)
                wait(act, "yo_d", g, 0)
                for c, t0, n in CHUNKS:
                    wait(act, "dd", g, 4 * c + 4)
                    nc.scalar.activation(dec[0:n, :, 0:n], dec[0:n, :, 0:n], ACT.Exp).then_inc(sems["de"], 1)
                    if c:
                        wait(act, "sd", g, 2 * c)
                        wait(act, "cs", g, c)
                    nc.scalar.activation(El[:, :, 0:n], csr[:, :, t0:t0 + n], ACT.Exp).then_inc(sems["el"], 1)
                    wait(act, "d4", g, c + 1)
                    nc.scalar.activation(de4[0:n, :], de4[0:n, :], ACT.Exp).then_inc(sems["e4"], 1)
                for k in range(4):
                    wait(act, "h0_t", g, k + 1)
                    wait(act, "ys_t", g, max(k - 1, 0))
                    nc.scalar.activation(h0T[:, k % 2, :], X[k % 2][:, :], ACT.Copy).then_inc(sems["h0_c"], 1)
                wait(act, "ps_t", g, 1)
                wait(act, "p_out", g, 0)
                nc.scalar.activation(Sout[:, :, :], Y[:, 0:2 * P].rearrange("p (j n) -> p j n", j=2), ACT.Copy).then_inc(sems["ps_c"], 1)
                wait(act, "ps_c", g, 1)
                pst = A["p_ssm"][0, 0].rearrange("(g j h) p n -> g j (h p) n", g=SG, j=2)
                sst = A["s_ssm"][0].rearrange("b (g j h) p n -> g j (h p) b n", g=SG, j=2)
                for j in range(2):
                    act.dma_start(pst[ds(g, 1)][0:1, j].rearrange("a q n -> (a q) n"), Sout[:, j, :]).then_inc(sems["p_out"], 16)
                wait(act, "yg", g, 1)
                wait(act, "ss_t", g, 0)
                nc.scalar.activation(ysq[:, :, :], yT[:, :, :], ACT.Square).then_inc(sems["sq"], 1)
                wait(act, "sn_a", g, 4)
                for j in range(2):
                    act.dma_start(sst[ds(g, 1)][0:1, j].rearrange("a q b n -> (a q) b n"), h0[:, j, :, :]).then_inc(sems["s_out"], 16)
                wait(act, "ss_t", g, 1)
                wait(act, "yr", g, 0)
                for half, bank in enumerate((Y, Z)):
                    nc.scalar.activation(rst[:, half * HALF:(half + 1) * HALF], bank[:, 0:HALF], ACT.Sqrt,
                                         bias=eps[:, :], scale=1.0 / (2 * P)).then_inc(sems["rt"], 1)
                wait(act, "yn", g, 2)
                act.dma_start(S["ynT"][ds(g * 2 * P, 2 * P), :].rearrange("(j p) t -> p j t", p=P), yT[:, :, :]).then_inc(sems["y_out"], 16)

        @block.tensor
        def _(pe):
            ident = per["ident"]
            pe.wait_ge(pre_d, 5)
            for t, t0, n in CHUNKS:
                nc.tensor.transpose(Y[0:n, t * SH:(t + 1) * SH], dtv[:, t0:t0 + n], ident[0:SH, 0:SH])
            for t, t0, n in CHUNKS:
                mm = nc.tensor.transpose(Z[0:n, t * SH:(t + 1) * SH], csv[:, t0:t0 + n], ident[0:SH, 0:SH])
            mm.then_inc(pre_t, 1)
            pe.wait_ge(pre_d, 9)
            pe.wait_ge(const_set, 3)
            with pe.Fori(0, SG) as g:
                wait(pe, "stc_in", g, 48)
                wait(pe, "sn_a", g, 0)
                pe.sem_inc(pe_step, 1)
                for q in range(4):
                    mm = nc.tensor.transpose(X[0][:, q * 24:(q + 1) * 24], stc[:, q, :], ident[0:24, 0:24])
                mm.then_inc(sems["st_t"], 1)
                wait(pe, "sel_d", g, 2)
                for q in range(4):
                    mm = nc.tensor.transpose(X[1][0:27, q * P:(q + 1) * P], sel[:, q, :], ident[:, :])
                mm.then_inc(sems["sel_t"], 1)
                wait(pe, "xa_s", g, 1)
                for t, t0, n in CHUNKS:
                    if t == 0:
                        wait(pe, "ext_s", g, 2)
                    elif t == 1:
                        wait(pe, "sel_c", g, 1)
                    else:
                        wait(pe, "xd", g, t - 1)
                        wait(pe, "bt", g, t - 1)
                    pe.sem_inc(pe_step, 1)
                    for q in range(3):
                        mm = nc.tensor.transpose(X[t % 2][0:n, q * P:(q + 1) * P], xa[:, q, t0:t0 + n], ident[:, :])
                    mm.then_inc(sems["tt"], 1)

                def cb(c):
                    _, t0, n = CHUNKS[c]
                    if c < 2:
                        wait(pe, "xd", g, 5)
                        wait(pe, "bt", g, 5)
                    else:
                        wait(pe, "cb_m", g, c - 1)
                    nc.tensor.matmul(X[c % 2][0:n, 0:n], xa[:, 2, t0:t0 + n], xa[:, 3, t0:t0 + n], start=True,
                                     stop=True).then_inc(sems["cb_t"], 1)

                cb(0)
                wait(pe, "rt", g, 0)
                for c, t0, n in CHUNKS:
                    if c < 4:
                        cb(c + 1)
                    wait(pe, "md", g, c + 1)
                    if c < 4:
                        wait(pe, "cs", g, c + 1)
                        wait(pe, "sd", g, 2 * c)
                        wait(pe, "s0", g, 1)
                    wait(pe, "yd", g, 2 * c)
                    pe.sem_inc(pe_step, 1)
                    for h in range(4):
                        out = Y[64 * (h % 2):64 * (h % 2) + 64, (h // 2) * P:(h // 2) * P + n]
                        mm = nc.tensor.matmul(out, xdt[0:n, c, h, :], dec[0:n, h, 0:n], start=True, stop=(c == 4))
                        if c < 4:
                            mm = nc.tensor.matmul(out, St[:, h * 64:(h + 1) * 64], Cs[:, h, :], start=False, stop=True)
                    mm.then_inc(sems["yt"], 1)
                    if c < 4:
                        wait(pe, "xe", g, c + 1)
                        nc.tensor.matmul(Z[:, 0:256], Bt[:, c, :], xde[:, :, :], start=True, stop=True).then_inc(sems["stt"], 1)
                wait(pe, "h0_in", g, 32)
                wait(pe, "sd", g, 8)

                def carried(k):
                    wait(pe, "h0_c", g, k + 1)
                    j = k // 2
                    for i in range(4):
                        b = 4 * (k % 2) + i
                        mm = nc.tensor.matmul(Z[:, j * SAMP + b * NT:j * SAMP + (b + 1) * NT], h0T[:, k % 2, i * P:(i + 1) * P],
                                              xa[:, 3, SEQ + b * NT:SEQ + (b + 1) * NT], start=True, stop=True)
                    mm.then_inc(sems["ys_t"], 1)

                for k in range(4):
                    if k < 2:
                        wait(pe, "cb_m", g, 5)
                    else:
                        wait(pe, "h0_c", g, k - 1)
                    for i in range(4):
                        mm = nc.tensor.transpose(X[k % 2][:, i * P:(i + 1) * P], h0[:, k // 2, 4 * (k % 2) + i, :], ident[:, :])
                    mm.then_inc(sems["h0_t"], 1)
                    if k:
                        carried(k - 1)
                carried(3)
                wait(pe, "yd", g, 10)
                for j in range(2):
                    mm = nc.tensor.transpose(Y[:, j * P:(j + 1) * P], St[:, j * P:(j + 1) * P], ident[:, :])
                mm.then_inc(sems["ps_t"], 1)
                wait(pe, "xe", g, 5)
                wait(pe, "bm", g, 1)
                for k in range(4):
                    wait(pe, "h0_c", g, 4)
                    if k >= 2:
                        wait(pe, "sn_a", g, k - 1)
                    j, half = k // 2, k % 2
                    nc.tensor.matmul(X[k % 2][:, :], xde[0:SAMP, 2 * j:2 * j + 2, :].rearrange("p h q -> p (h q)"),
                                     Bm[:, 4 * half:4 * half + 4, :].rearrange("p b n -> p (b n)"),
                                     start=True, stop=True).then_inc(sems["sn_t"], 1)
                wait(pe, "sq", g, 1)
                wait(pe, "ps_c", g, 1)
                wait(pe, "yo_d", g, 4)
                for half, bank in enumerate((Y, Z)):
                    for j in range(2):
                        mm = nc.tensor.matmul(bank[:, 0:HALF], ones[:, :], ysq[:, j, half * HALF:(half + 1) * HALF],
                                              start=(j == 0), stop=(j == 1))
                mm.then_inc(sems["ss_t"], 1)

        @block.vector
        def _(dve):
            TT, TS, STT = nc.vector.tensor_tensor, nc.vector.tensor_scalar, nc.vector.scalar_tensor_tensor
            dve.wait_ge(pre_in, 16 * 9)
            TS(dr[:, :], dr[:, :], hv[:, 0:1], None, ALU.add).then_inc(pre_d, 1)
            dve.wait_ge(pre_d, 1)
            STT(dn[:, :], dr[:, :], -1.0, dr[:, :], ALU.mult, ALU.min).then_inc(pre_d, 1)
            dve.wait_ge(pre_a, 3)
            STT(dtv[:, :], dr[:, :], 0.0, dn[:, :], ALU.max, ALU.add).then_inc(pre_d, 1)
            dve.wait_ge(pre_d, 3)
            TS(dn[:, :], dtv[:, :], hv[:, 2:3], -1.0, ALU.mult, ALU.mult).then_inc(pre_d, 1)
            dve.wait_ge(pre_d, 4)
            nc.vector.tensor_tensor_scan(csv[:, :], seg[:, :], dn[:, :], 0.0, ALU.mult, ALU.add).then_inc(pre_d, 1)
            dve.wait_ge(pre_t, 1)
            for dst, bank in ((dtt, Y), (cst, Z)):
                nc.vector.tensor_copy(dst[:, 0:4, :], bank[:, 0:4 * SH].rearrange("p (t h) -> p t h", t=4)).then_inc(pre_d, 1)
                nc.vector.tensor_copy(dst[0:SAMP, 4, :], bank[0:SAMP, 4 * SH:5 * SH]).then_inc(pre_d, 1)
            dve.wait_ge(const_set, 3)
            with dve.Fori(0, SG) as g:
                wait(dve, "st_t", g, 1)
                wait(dve, "exs_in", g, 48)
                wait(dve, "ext_in", g, 48)
                wait(dve, "sel_d", g, 0)
                wait(dve, "cv", g, 0)
                TC = nc.vector.tensor_copy
                TC(extS[:, :, :, 0:3], X[0][:, 0:96].rearrange("p (q b k) -> p q b k", q=4, k=3)).then_inc(sems["ext_s"], 1)
                TC(extS[:, :, :, 3:11], exs[:, :, :].rearrange("p q (b t) -> p q b t", t=NT)).then_inc(sems["ext_s"], 1)
                wait(dve, "ext_s", g, 2)
                wait(dve, "sel_t", g, 0)
                TC(sel[:, :, 0:3], ext[:, :, SEQ:SEQ + 3]).then_inc(sems["sel_d"], 1)
                TC(sel[:, :, 3:27].rearrange("p q (b k) -> p q b k", k=3), extS[:, :, :, NT:NT + 3]).then_inc(sems["sel_d"], 1)
                wait(dve, "loc", g, 12)
                wait(dve, "ys_t", g, 0)
                wait(dve, "yt", g, 0)
                wait(dve, "yd", g, 0)
                for kk in range(CW):
                    if kk:
                        wait(dve, "cv", g, 8 * kk)
                        wait(dve, "sel_d", g, 2)
                    for q in range(4):
                        w = cwl[:, kk, q:q + 1]
                        for out, src in ((xa[:, q, 0:SEQ], ext[:, q, kk:kk + SEQ]),
                                         (xa[:, q, SEQ:TOK].rearrange("p (b t) -> p b t", t=NT), extS[:, q, :, kk:kk + NT])):
                            if kk == 0:
                                TS(out, src, w, cwl[:, CW, q:q + 1], ALU.mult, ALU.add).then_inc(sems["cv"], 1)
                            else:
                                STT(out, src, w, out, ALU.mult, ALU.add).then_inc(sems["cv"], 1)
                wait(dve, "ps_t", g, 0)
                nc.vector.memset(St[:, :], 0.0).then_inc(sems["s0"], 1)
                wait(dve, "xe", g, 0)
                for t, _, n in CHUNKS:
                    wait(dve, "tt", g, t + 1)
                    TT(xdt[0:n, t, :, :], X[t % 2][0:n, 0:256].rearrange("p (h q) -> p h q", h=4),
                       dtg[0:n, t, :].unsqueeze(2).broadcast_to((n, 4, 64)), ALU.mult).then_inc(sems["xd"], 1)
                wait(dve, "csr_in", g, 16)
                wait(dve, "y_out", g, 0)
                for c, t0, n in CHUNKS:
                    cols = slice(t0, t0 + n)
                    wait(dve, "yt", g, c)
                    for h in range(4):
                        TS(dec[0:n, h, 0:n], csr[0:n, h, cols], csg[0:n, c, h:h + 1], 0.0, ALU.subtract, ALU.min).then_inc(sems["dd"], 1)
                    wait(dve, "xe", g, c)
                    if c < 4:
                        TT(de4[:, :], csr[:, :, t0 + n - 1], csg[:, c, :], ALU.subtract).then_inc(sems["d4"], 1)
                    else:
                        wait(dve, "lm", g, 0)
                        TT(lastm[:, :, :], csr[0:SAMP, :, SEQ + NT - 1:TOK:NT], owner[:, :].unsqueeze(1).broadcast_to((SAMP, 4, NB)),
                           ALU.mult).then_inc(sems["lm"], 1)
                        wait(dve, "lm", g, 1)
                        nc.vector.tensor_reduce(de4[0:SAMP, :], lastm[:, :, :], AX, ALU.add).then_inc(sems["lm"], 1)
                        wait(dve, "lm", g, 2)
                        TT(de4[0:SAMP, :], de4[0:SAMP, :], csg[0:SAMP, 4, :], ALU.subtract).then_inc(sems["d4"], 1)
                    wait(dve, "cb_t", g, c + 1)
                    wait(dve, "md", g, c)
                    mask = causal if c < 4 else blockm
                    TT(CBm[0:n, 0:n], X[c % 2][0:n, 0:n], mask[:, :], ALU.mult).then_inc(sems["cb_m"], 1)
                    wait(dve, "de", g, c + 1)
                    wait(dve, "cb_m", g, c + 1)
                    TT(dec[0:n, :, 0:n], dec[0:n, :, 0:n], CBm[0:n, 0:n].unsqueeze(1).broadcast_to((n, 4, n)), ALU.mult).then_inc(sems["md"], 1)
                    wait(dve, "el", g, c + 1)
                    if c < 4:
                        TT(Cs[:, :, :], El[:, :, :], xa[:, 3, cols].unsqueeze(1).broadcast_to((P, 4, P)), ALU.mult).then_inc(sems["cs"], 1)
                    wait(dve, "e4", g, c + 1)
                    if c:
                        wait(dve, "stt", g, c)
                    else:
                        wait(dve, "sn_t", g, 0)
                    TT(xde[0:n, :, :], xdt[0:n, c, :, :], de4[0:n, :].unsqueeze(2).broadcast_to((n, 4, 64)), ALU.mult).then_inc(sems["xe"], 1)
                    wait(dve, "yt", g, c + 1)
                    for j in range(2):
                        STT(yT[:, j, cols], xa[:, j, cols], dkl[:, j:j + 1], Y[:, j * P:j * P + n], ALU.mult, ALU.add).then_inc(sems["yd"], 1)
                    if c < 4:
                        sv = St[:, :].rearrange("p (h q) -> p h q", h=4)
                        if c:
                            wait(dve, "sd", g, 2 * c)
                        wait(dve, "s0", g, 1)
                        TT(sv, sv, El[:, :, n - 1:n].broadcast_to((P, 4, 64)), ALU.mult).then_inc(sems["sd"], 1)
                        wait(dve, "sd", g, 2 * c + 1)
                        wait(dve, "stt", g, c + 1)
                        TT(St[:, :], St[:, :], Z[:, 0:256], ALU.add).then_inc(sems["sd"], 1)
                wait(dve, "ys_t", g, 4)
                wait(dve, "ya", g, 0)
                for j in range(2):
                    for hh in range(2):
                        part = slice(64 * hh, 64 * hh + 64)
                        TT(yo[part, j, :], Z[part, j * SAMP:(j + 1) * SAMP], El[part, 2 * j + hh, 0:SAMP], ALU.mult).then_inc(sems["yo_d"], 1)
                wait(dve, "yo_d", g, 4)
                wait(dve, "yd", g, 10)
                TT(yT[:, :, SEQ:TOK], yT[:, :, SEQ:TOK], yo[:, :, :], ALU.add).then_inc(sems["ya"], 1)
                wait(dve, "ya", g, 1)
                wait(dve, "zb_s", g, 1)
                TT(yT[:, :, :], yT[:, :, :], zb[:, :, :], ALU.mult).then_inc(sems["yg"], 1)
                wait(dve, "sn_m", g, 4)
                for k in range(4):
                    wait(dve, "sn_t", g, k + 1)
                    hv4 = h0[:, k // 2, 4 * (k % 2):4 * (k % 2) + 4, :].rearrange("p b n -> p (b n)")
                    TT(hv4, hv4, X[k % 2][:, :], ALU.add).then_inc(sems["sn_a"], 1)
                wait(dve, "rt", g, 2)
                nc.vector.reciprocal(rst[:, :], rst[:, :]).then_inc(sems["ri"], 1)
                wait(dve, "ri", g, 1)
                TT(yT[:, :, :], yT[:, :, :], rst[:, :].unsqueeze(1).broadcast_to((P, 2, TOK)), ALU.mult).then_inc(sems["yr"], 1)
                wait(dve, "yr", g, 1)
                for j in range(2):
                    TS(yT[:, j, :], yT[:, j, :], gvl[:, j:j + 1], None, ALU.mult).then_inc(sems["yn"], 1)



def phase_pa(nc, A, S, per):
    KA = AW // P
    NB_A = D // BC
    with ExitStack() as ctx:
        m = Mem(nc, ctx)
        g = Gemm(nc, m, KA, "a")
        oF = m.sb("oaF", [P, 4, TOK])
        oH = m.sb("oaH", [P, KA, TOK], F32R)
        oL = m.sb("oaL", [P, KA, TOK], F32R)
        r = m.sb("ra", [P, 2, TOK])
        o_in = [m.sem(f"o_in{i}") for i in range(4)]
        r_in = [m.sem(f"ra_in{i}") for i in range(2)]
        o_hi, o_lo, r_s = m.sem("o_hi"), m.sem("o_lo"), m.sem("ra_s")
        block = ctx.enter_context(nc.Block())
        wv = A["w_o_a"][0].rearrange("(k p) n -> p k n", p=P)

        @block.sync
        def _(sp):
            for n in range(NB_A):
                g.load(sp, n, n % 3, wv[:, :, n * BC:(n + 1) * BC])
                if n == 0:
                    for k in range(KA):
                        if k >= 4:
                            sp.wait_ge(o_lo, k - 3)
                        sp.dma_start(oF[:, k % 4, :], S["oaT"][k * P:(k + 1) * P, :]).then_inc(o_in[k % 4], 16)
                for u in (2 * n, 2 * n + 1):
                    sp.wait_ge(g.stored[u % 2], (u // 2) * 16)
                    sp.dma_start(r[:, u % 2, :], S["projT"][COL_R + u * P:COL_R + (u + 1) * P, :]).then_inc(r_in[u % 2], 16)
            for c in range(2):
                sp.wait_ge(g.stored[c], NB_A * 16)

        @block.gpsimd
        def _(pool):
            pool.sem_inc(g.lo, 6)
            for u in range(2 * NB_A):
                g.low(pool, (u // 2) % 3, u % 2, u)

        @block.scalar
        def _(act):
            def sigmoid(u):
                act.wait_ge(r_in[u % 2], (u // 2) * 16 + 16)
                nc.scalar.activation(r[:, u % 2, :], r[:, u % 2, :], ACT.Sigmoid).then_inc(r_s, 1)

            def store(u):
                act.wait_ge(g.evac, u + 3)
                act.dma_start(S["maT"][u * P:(u + 1) * P, :], g.ev[:, u % 2, :]).then_inc(g.stored[u % 2], 16)

            g.high(act, 0, 0, 0, 0)
            for k in range(KA):
                act.wait_ge(o_in[k % 4], (k // 4) * 16 + 16)
                nc.scalar.activation(oH[:, k, :], oF[:, k % 4, :], ACT.Copy).then_inc(o_hi, 1)
            for u in range(2 * NB_A):
                if u + 1 < 2 * NB_A:
                    g.high(act, ((u + 1) // 2) % 3, (u + 1) // 6, (u + 1) % 2, u + 1)
                sigmoid(u)
                if u:
                    store(u - 1)
            store(2 * NB_A - 1)

        @block.tensor
        def _(pe):
            pe.sem_inc(g.used, 2)
            pe.wait_ge(o_lo, KA)
            for u in range(2 * NB_A):
                for half in range(2):
                    g.multiply(pe, u % 2, u, oH, oL, half)

        @block.vector
        def _(dve):
            dve.sem_inc(g.evac, 2)
            for k in range(KA):
                dve.wait_ge(o_hi, k + 1)
                nc.vector.tensor_tensor(oL[:, k, :], oF[:, k % 4, :], oH[:, k, :].bitcast(F32),
                                        ALU.subtract).then_inc(o_lo, 1)
            for u in range(2 * NB_A):
                dve.wait_ge(g.used, u + 3)
                dve.wait_ge(r_s, u + 1)
                dve.wait_ge(g.stored[u % 2], (u // 2) * 16)
                nc.vector.tensor_tensor(g.ev[:, u % 2, :].rearrange("p (a n) -> p a n", a=2),
                                        g.acc[u % 2][:, :, 0:HALF],
                                        r[:, u % 2, :].rearrange("p (a n) -> p a n", a=2), ALU.mult).then_inc(g.evac, 1)


def phase_out(nc, A, S, per):
    NU = D // P
    NBO = D // BC
    with ExitStack() as ctx:
        m = Mem(nc, ctx)
        g = Gemm(nc, m, KT, "o")
        aH = m.sb("aH", [P, KT, TOK], F32R)
        aL = m.sb("aL", [P, KT, TOK], F32R)
        big = m.sb("big", [P, 5 * D])
        out = big[:, :].rearrange("p (t d) -> p t d", t=5)
        mF = big[:, 0:KT * TOK].rearrange("p (k t) -> p k t", k=KT)
        rb = m.sb("rb", [P, 2, TOK])
        ssq = m.sb("ssq_o", [P, 5, 4])
        stat = m.sb("stat_o", [P, 5, 3])
        eps = m.sb("eps_o", [P, 1])
        pT = [m.ps(f"ps_o{i}", (P, 1024)) for i in range(2)]
        y_in, eps_set = m.sem("y_in"), m.sem("eps_seto")
        a_hi, a_lo = m.sem("a_hi"), m.sem("a_lo")
        rb_in = [m.sem(f"rb_in{i}") for i in range(2)]
        ma_in = [m.sem(f"ma_in{i}") for i in range(2)]
        rb_s, mul, mrg, o_t, o_c, sq_d = (m.sem(n) for n in ("rb_s", "o_mul", "o_mrg", "o_t", "o_c", "sq_d"))
        st_d, st_r, st_i, fin_in, gg_d, y_s, y_d, y_out = (
            m.sem(n) for n in ("st_d", "st_r", "st_i", "fin_in", "gg_d", "y_s", "y_d", "yo_out"))
        x3_in, xs_in = m.sem("x3_in"), m.sem("xs_in")
        block = ctx.enter_context(nc.Block())
        wb = A["w_o_b"][0].rearrange("(k p) n -> p k n", p=P)
        wo = A["w_o"][0].rearrange("(k p) n -> p k n", p=P)
        wide = g.raw[:, :, :, :].rearrange("p s k n -> p (s k n)")
        gpost, gateP, gateS = wide[:, 0:D], wide[:, D:2 * D], wide[:, 2 * D:3 * D]
        junk = rb[:, :, :].rearrange("p a t -> p (a t)")
        xT = [wide[:, (3 + t) * D:(4 + t) * D] for t in range(3)] + [gpost, wide[:, 3 * D:4 * D]]

        @block.sync
        def _(sp):
            g.load(sp, 0, 0, wb[:, :, 0:BC])
            for k in range(KT):
                sp.dma_start(mF[:, k, :], S["ynT"][k * P:(k + 1) * P, :]).then_inc(y_in, 16)
            for n in range(1, 2 * NBO):
                src = wb if n < NBO else wo
                g.load(sp, n, n % 3, src[:, :, (n % NBO) * BC:(n % NBO + 1) * BC])
                for u in (2 * n - 2, 2 * n - 1):
                    if u < NU:
                        if u >= 2:
                            sp.wait_ge(mrg, u - 1)
                        sp.dma_start(rb[:, u % 2, :], S["projT"][COL_R + D + u * P:COL_R + D + (u + 1) * P, :]
                                     ).then_inc(rb_in[u % 2], 16)
                        sp.dma_start(g.ev[:, u % 2, :], S["maT"][u * P:(u + 1) * P, :]).then_inc(ma_in[u % 2], 16)
            sp.wait_ge(g.lo, 6 + 2 * NU)
            sp.dma_start(gpost, A["g_post"][0:1, :].to_broadcast((P, D))).then_inc(fin_in, 16)
            sp.dma_start(gateP, S["gate"][0:1, :].to_broadcast((P, D))).then_inc(fin_in, 16)
            for b in range(NB):
                sp.dma_start(gateS[b * NT:(b + 1) * NT, :], S["gate"][b + 1:b + 2, :].to_broadcast((NT, D))).then_inc(fin_in, 16)
            for t in range(3):
                sp.dma_start(xT[t], A["x_prompt"][0, t * P:(t + 1) * P, :]).then_inc(fin_in, 16)
            sp.wait_ge(gg_d, 2)
            sp.dma_start(xT[3], A["x_prompt"][0, 3 * P:4 * P, :]).then_inc(x3_in, 16)
            for t in range(5):
                sp.wait_ge(y_d, t + 1)
                if t == 0:
                    sp.dma_start(xT[4][0:SAMP, :], A["x_sample"].rearrange("b t d -> (b t) d")).then_inc(xs_in, 16)
                dst = A["y_prompt"][0, t * P:(t + 1) * P, :] if t < 4 else A["y_sample"].rearrange("b t d -> (b t) d")
                n = P if t < 4 else SAMP
                sp.dma_start(dst, out[0:n, t, :]).then_inc(y_out, 16)
            sp.wait_ge(y_out, 5 * 16)

        @block.gpsimd
        def _(pool):
            nc.gpsimd.memset(eps[:, :], EPS).then_inc(eps_set, 1)
            pool.sem_inc(g.lo, 6)
            for u in range(2 * NU):
                g.low(pool, (u // 2) % 3, u % 2, u)

        @block.scalar
        def _(act):
            def high(u):
                g.high(act, (u // 2) % 3, u // 6, u % 2, u)

            def squares(q):
                act.wait_ge(o_c, 8 * q + 8)
                for t in range(5):
                    n = P if t < 4 else SAMP
                    if 5 * q + t:
                        act.wait_ge(sq_d, 5 * q + t)
                    nc.scalar.activation(junk[0:n, 0:4 * P], out[0:n, t, q * 4 * P:(q + 1) * 4 * P], ACT.Square,
                                         accum_out=ssq[0:n, t, q:q + 1]).then_inc(sq_d, 1)

            high(0)
            high(1)
            for k in range(KT):
                act.wait_ge(y_in, 16 * KT)
                nc.scalar.activation(aH[:, k, :], mF[:, k, :], ACT.Copy).then_inc(a_hi, 1)
            for u in range(NU):
                act.wait_ge(rb_in[u % 2], (u // 2) * 16 + 16)
                nc.scalar.activation(rb[:, u % 2, :], rb[:, u % 2, :], ACT.Sigmoid).then_inc(rb_s, 1)
                high(u + 2)
            act.wait_ge(g.used, 2 + NU)
            for k in range(KT):
                act.wait_ge(mrg, k + 1)
                nc.scalar.activation(aH[:, k, :], mF[:, k, :], ACT.Copy).then_inc(a_hi, 1)
            for v in range(NU):
                u = NU + v
                if u + 2 < 2 * NU:
                    high(u + 2)
                act.wait_ge(g.used, u + 3)
                if v >= 2:
                    act.wait_ge(o_t, v - 1)
                nc.scalar.activation(g.ev[:, u % 2, :].rearrange("p (a n) -> p a n", a=2),
                                     g.acc[u % 2][:, :, 0:HALF], ACT.Copy).then_inc(g.evac, 1)
                if v % 4 == 1 and v > 4:
                    squares(v // 4 - 1)
            squares(3)
            act.wait_ge(st_d, 1)
            act.wait_ge(eps_set, 1)
            nc.scalar.activation(stat[:, :, 1], stat[:, :, 0], ACT.Sqrt, bias=eps[:, :], scale=1.0 / D).then_inc(st_r, 1)

        @block.tensor
        def _(pe):
            ident = per["ident"]
            pe.sem_inc(g.used, 2)
            pe.wait_ge(a_lo, KT)

            def back(v):
                pe.wait_ge(g.evac, NU + v + 3)
                if v >= 2:
                    pe.wait_ge(o_c, 2 * (v - 1))
                for t in range(5):
                    n = P if t < 4 else SAMP
                    mm = nc.tensor.transpose(pT[v % 2][0:n, t * P:(t + 1) * P], g.ev[:, v % 2, t * P:t * P + n], ident[:, :])
                mm.then_inc(o_t, 1)

            for u in range(2 * NU):
                if u == NU:
                    pe.wait_ge(a_lo, 2 * KT)
                for half in range(2):
                    g.multiply(pe, u % 2, u, aH, aL, half)
                if u > NU:
                    back(u - NU - 1)
            back(NU - 1)

        @block.vector
        def _(dve):
            TT = nc.vector.tensor_tensor

            def low(k):
                TT(aL[:, k % KT, :], mF[:, k % KT, :], aH[:, k % KT, :].bitcast(F32), ALU.subtract).then_inc(a_lo, 1)

            dve.sem_inc(g.evac, 2)
            for k in range(KT):
                dve.wait_ge(a_hi, k + 1)
                low(k)
            nc.vector.memset(ssq[:, :, :], 0.0)
            dve.wait_ge(a_lo, KT)
            for u in range(NU):
                dve.wait_ge(g.used, u + 3)
                dve.wait_ge(rb_s, u + 1)
                dve.wait_ge(ma_in[u % 2], (u // 2) * 16 + 16)
                TT(mF[:, u, :].rearrange("p (a n) -> p a n", a=2), g.acc[u % 2][:, :, 0:HALF],
                   rb[:, u % 2, :].rearrange("p (a n) -> p a n", a=2), ALU.mult).then_inc(g.evac, 1)
                dve.wait_ge(g.evac, u + 3)
                TT(mF[:, u, :], mF[:, u, :], g.ev[:, u % 2, :], ALU.add).then_inc(mrg, 1)
            for k in range(KT):
                dve.wait_ge(a_hi, KT + k + 1)
                low(k)
            dve.wait_ge(a_lo, 2 * KT)
            for v in range(NU):
                dve.wait_ge(o_t, v + 1)
                cols = slice(v * P, (v + 1) * P)
                nc.vector.tensor_copy(out[:, 0:4, cols], pT[v % 2][:, 0:512].rearrange("p (t c) -> p t c", t=4)).then_inc(o_c, 1)
                nc.vector.tensor_copy(out[0:SAMP, 4, cols], pT[v % 2][0:SAMP, 512:640]).then_inc(o_c, 1)
            dve.wait_ge(fin_in, 16 * (5 + NB))
            TT(gateP, gateP, gpost, ALU.mult).then_inc(gg_d, 1)
            TT(gateS[0:SAMP, :], gateS[0:SAMP, :], gpost[0:SAMP, :], ALU.mult).then_inc(gg_d, 1)
            dve.wait_ge(sq_d, 20)
            nc.vector.tensor_reduce(stat[:, :, 0], ssq[:, :, :], AX, ALU.add).then_inc(st_d, 1)
            dve.wait_ge(st_r, 1)
            nc.vector.reciprocal(stat[:, :, 2], stat[:, :, 1]).then_inc(st_i, 1)
            dve.wait_ge(st_i, 1)
            dve.wait_ge(gg_d, 2)
            for t in range(5):
                n = P if t < 4 else SAMP
                gg = gateP if t < 4 else gateS
                nc.vector.scalar_tensor_tensor(out[0:n, t, :], out[0:n, t, :], stat[0:n, t, 2:3], gg[0:n, :],
                                               ALU.mult, ALU.mult).then_inc(y_s, 1)
                dve.wait_ge(y_s, t + 1)
                if t >= 3:
                    dve.wait_ge(x3_in if t == 3 else xs_in, 16)
                TT(out[0:n, t, :], out[0:n, t, :], xT[t][0:n, :], ALU.add).then_inc(y_d, 1)



NAMES = ("x_prompt", "x_sample", "cache_a_w128", "cache_a_w512", "cache_a_w2048", "state_conv", "state_ssm",
         "c_prompt", "c_sample", "w_ada", "b_ada", "g_pre", "g_post", "w_in", "conv_w", "conv_b", "dt_bias", "a_log",
         "d_skip", "g_ssm", "w_o_a", "w_o_b", "w_o")
OUTS = (("y_prompt", (1, SEQ, D)), ("y_sample", (NB, NT, D)),
        ("p_kv128", (1, 1, 128, 2, H, E)), ("p_kv512", (1, 1, 512, 2, H, E)), ("p_kv2048", (1, 1, 512, 2, H, E)),
        ("p_conv", (1, 1, CW - 1, CONV)), ("p_ssm", (1, 1, SH, 64, 128)),
        ("s_kv128", (1, NB, 128, 2, H, E)), ("s_kv512", (1, NB, 512, 2, H, E)), ("s_kv2048", (1, NB, 2048, 2, H, E)),
        ("s_conv", (1, NB, CW - 1, CONV)), ("s_ssm", (1, NB, SH, 64, 128)))


def build(nc, A, phases=9):
    S = {"gate": nc.dram_tensor("gate", (NSEQ, D), F32).ap(),
         "projT": nc.dram_tensor("projT", (INW, TOK), F32).ap(),
         "csT": nc.dram_tensor("csT", (SH, TOK), F32).ap(),
         "ynT": nc.dram_tensor("ynT", (D, TOK), F32).ap(),
         "maT": nc.dram_tensor("maT", (D, TOK), F32).ap(),
         "oaT": nc.dram_tensor("oaT", (AW, TOK), F32).ap(),
         "kvtok": nc.dram_tensor("kvtok", (TOK, P + 3 * QKV), F32).ap()}
    with ExitStack() as keep:
        k = Mem(nc, keep)
        per = {"ident": k.sb("ident_sb", [P, P]), "vec": k.sb("vec", [P, 240]), "oS": k.sb("oS", [P, H, SAMP])}
        with ExitStack() as early:
            e = Mem(nc, early)
            per["hH"] = e.sb("hH", [P, KT, TOK], F32R)
            per["hL"] = e.sb("hL", [P, KT, TOK], F32R)
            phase_norm(nc, A, S, per)
            if phases > 1:
                phase_proj(nc, A, S, per)
        if phases > 2:
            phase_ssm(nc, A, S, per)
        if phases > 3:
            phase_pa(nc, A, S, per)
            phase_out(nc, A, S, per)


def kernel(**inputs):
    import numpy as np
    import concourse.bacc as bacc
    from concourse.bass_utils import run_bass_kernel_spmd

    nc = bacc.Bacc("TRN2", target_bir_lowering=False, num_devices=1)
    arrays, A = {}, {}
    for name in NAMES:
        arrays[f"in_{name}"] = np.ascontiguousarray(inputs[name])
    for name, a in shape_constants().items():
        arrays[f"in_{name}"] = a
    for name, a in arrays.items():
        A[name[3:]] = nc.dram_tensor(name, a.shape, mybir.dt.from_np(a.dtype), kind="ExternalInput").ap()
    for name, shape in OUTS:
        A[name] = nc.dram_tensor(f"out_{name}", shape, F32, kind="ExternalOutput").ap()
    build(nc, A)
    got = run_bass_kernel_spmd(nc, [arrays], core_ids=[0]).results[0]
    return tuple(got[f"out_{name}"] for name, _ in OUTS)
```
